# Optimizing a Trainium2 kernel written in Bass

```python
import math
import jax, jax.numpy as jnp
from jax import lax
import numpy as np

D_MODEL = 2048
BATCH = 1
SEQ = 512
DEPTH = 1

GLA_WIDTH = D_MODEL // 2
GLA_HEADS = 4
GLA_DK = (GLA_WIDTH // 2) // GLA_HEADS
GLA_DV = GLA_WIDTH // GLA_HEADS
GLA_GATE_RANK = 16
GLA_TAU = 16.0
GLA_CHUNK = 64
ATT_WIDTH = D_MODEL - GLA_WIDTH
ATT_HEADS = 8
ATT_HD = ATT_WIDTH // ATT_HEADS
DILATED_BRANCHES = ((128, 1), (512, 4), (2048, 16))
BAND_BLOCK = 128
ROPE_THETA = 10000.0
D_FF = 5632
CONV_WIDTH = 3
DEEPNORM_ALPHA = (2.0 * DEPTH) ** 0.25
DEEPNORM_BETA = (8.0 * DEPTH) ** -0.25
ADA_STD = 0.005
LN_EPS = 1e-5
RMS_EPS = 1e-6
MAX_POS_OFFSET = 1024
IN_SIZES = (GLA_HEADS * GLA_DK, GLA_HEADS * GLA_DK, GLA_WIDTH, GLA_WIDTH, GLA_GATE_RANK,
            ATT_WIDTH, ATT_WIDTH, ATT_WIDTH)
IN_IS_VALUE = (False, False, True, False, False, False, False, True)
IN_COLS = sum(IN_SIZES)

kernel_name = "hymba_gla_longnet_convffn_deepnorm_adaln"

def split_sizes(t, sizes):
    out, start = [], 0
    for n in sizes:
        out.append(t[..., start:start + n])
        start += n
    return out

def layer_norm(x, g, b):
    xf = x.astype(jnp.float32)
    mu = jnp.mean(xf, axis=-1, keepdims=True)
    var = jnp.mean(jnp.square(xf - mu), axis=-1, keepdims=True)
    return ((xf - mu) * lax.rsqrt(var + LN_EPS) * g.astype(jnp.float32) + b.astype(jnp.float32)).astype(x.dtype)

def rotary(t, positions):
    half = t.shape[-1] // 2
    inv_freq = ROPE_THETA ** (-jnp.arange(half, dtype=jnp.float32) / half)
    ang = positions.astype(jnp.float32)[..., None] * inv_freq
    cos = jnp.cos(ang)[:, :, None, :]
    sin = jnp.sin(ang)[:, :, None, :]
    t1 = t[..., :half].astype(jnp.float32)
    t2 = t[..., half:].astype(jnp.float32)
    return jnp.concatenate([t1 * cos - t2 * sin, t2 * cos + t1 * sin], axis=-1).astype(t.dtype)

def gla_chunked(q, k, v, log_a):
    B, S, H, dk = q.shape
    dv = v.shape[-1]
    nc = S // GLA_CHUNK

    def chunks(t):
        return t.reshape(B, nc, GLA_CHUNK, H, t.shape[-1]).transpose(1, 0, 3, 2, 4)

    causal = jnp.tril(jnp.ones((GLA_CHUNK, GLA_CHUNK), dtype=bool))[:, :, None]

    def step(state, inp):
        qc, kc, vc, gc = inp
        b = jnp.cumsum(gc, axis=-2)
        diff = b[..., :, None, :] - b[..., None, :, :]
        decay = jnp.exp(jnp.where(causal, diff, -jnp.inf))
        scores = jnp.einsum('bhtd,bhsd,bhtsd->bhts', qc, kc, decay)
        o = jnp.einsum('bhts,bhse->bhte', scores, vc) \
            + jnp.einsum('bhtd,bhde->bhte', qc * jnp.exp(b), state)
        b_last = b[..., -1:, :]
        state = jnp.swapaxes(jnp.exp(b_last), -1, -2) * state \
            + jnp.einsum('bhsd,bhse->bhde', kc * jnp.exp(b_last - b), vc)
        return state, o

    state0 = jnp.zeros((B, H, dk, dv), jnp.float32)
    _, o = lax.scan(step, state0, (chunks(q), chunks(k), chunks(v), chunks(log_a)))
    return o.transpose(1, 0, 3, 2, 4).reshape(B, S, H, dv)

def banded_causal_attention(q, k, v, span):
    L, hd = q.shape[-2], q.shape[-1]
    nb = -(-L // BAND_BLOCK)
    lp = nb * BAND_BLOCK
    n_prev = -(-span // BAND_BLOCK)
    lead = [(0, 0)] * (q.ndim - 2)
    qb = jnp.pad(q, lead + [(0, lp - L), (0, 0)]).reshape(*q.shape[:-2], nb, BAND_BLOCK, hd)

    def with_history(t):
        t = jnp.pad(t, lead + [(n_prev * BAND_BLOCK, lp - L), (0, 0)])
        t = t.reshape(*t.shape[:-2], nb + n_prev, BAND_BLOCK, hd)
        return jnp.concatenate([t[..., j:j + nb, :, :] for j in range(n_prev + 1)], axis=-2)

    kb, vb = with_history(k), with_history(v)
    kw = (n_prev + 1) * BAND_BLOCK
    i = jnp.arange(BAND_BLOCK)[None, :, None]
    m = jnp.arange(kw)[None, None, :]
    blk = jnp.arange(nb)[:, None, None]
    dist = i + n_prev * BAND_BLOCK - m
    key_pos = (blk - n_prev) * BAND_BLOCK + m
    mask = (dist >= 0) & (dist <= span) & (key_pos >= 0)

    s = jnp.einsum('...nid,...nmd->...nim', qb.astype(jnp.float32), kb.astype(jnp.float32))
    s = jnp.where(mask, s, -jnp.inf)
    lse = jax.nn.logsumexp(s, axis=-1)
    p = jnp.exp(s - lse[..., None])
    o = jnp.einsum('...nim,...nmd->...nid', p, vb.astype(jnp.float32))
    o = o.reshape(*q.shape[:-2], lp, hd)[..., :L, :]
    lse = lse.reshape(*q.shape[:-2], lp)[..., :L]
    return o, lse

def dilated_attention(q, k, v):
    B, H, S, hd = q.shape
    q = q * (hd ** -0.5)
    outs, lses = [], []
    for window, dil in DILATED_BRANCHES:
        def to_sub(t):
            return jnp.swapaxes(t.reshape(B, H, S // dil, dil, hd), 2, 3)
        o, lse = banded_causal_attention(to_sub(q), to_sub(k), to_sub(v), window // dil)
        outs.append(jnp.swapaxes(o, 2, 3).reshape(B, H, S, hd))
        lses.append(jnp.swapaxes(lse, 2, 3).reshape(B, H, S))
    w = jax.nn.softmax(jnp.stack(lses, axis=0), axis=0)
    return jnp.einsum('rbhs,rbhsd->bhsd', w, jnp.stack(outs, axis=0))

def token_mixer(u, positions, w_in, w_gla_gate, b_gla_gate, gla_norm_g, w_out):
    B, S, _ = u.shape
    proj = u @ w_in
    gq, gk, gv, gr, glr, aq, ak, av = split_sizes(proj, IN_SIZES)
    f32 = jnp.float32
    q_g = gq.astype(f32).reshape(B, S, GLA_HEADS, GLA_DK) * (GLA_DK ** -0.5)
    k_g = gk.astype(f32).reshape(B, S, GLA_HEADS, GLA_DK)
    v_g = gv.astype(f32).reshape(B, S, GLA_HEADS, GLA_DV)
    gate_logits = glr.astype(f32) @ w_gla_gate.astype(f32) + b_gla_gate.astype(f32)
    log_a = (jax.nn.log_sigmoid(gate_logits) / GLA_TAU).reshape(B, S, GLA_HEADS, GLA_DK)
    o_g = gla_chunked(q_g, k_g, v_g, log_a)
    o_g = o_g * lax.rsqrt(jnp.mean(jnp.square(o_g), axis=-1, keepdims=True) + RMS_EPS) \
        * gla_norm_g.astype(f32)
    o_g = (o_g.reshape(B, S, GLA_WIDTH) * jax.nn.silu(gr.astype(f32))).astype(u.dtype)
    q_a = rotary(aq.reshape(B, S, ATT_HEADS, ATT_HD), positions)
    k_a = rotary(ak.reshape(B, S, ATT_HEADS, ATT_HD), positions)
    v_a = av.reshape(B, S, ATT_HEADS, ATT_HD)
    o_a = dilated_attention(jnp.swapaxes(q_a, 1, 2), jnp.swapaxes(k_a, 1, 2), jnp.swapaxes(v_a, 1, 2))
    o_a = jnp.swapaxes(o_a, 1, 2).reshape(B, S, ATT_WIDTH).astype(u.dtype)
    return jnp.concatenate([o_g, o_a], axis=-1) @ w_out

def conv_ffn(u, w_up, conv_w, conv_b, w_down):
    S = u.shape[1]
    h = u @ w_up
    hp = jnp.pad(h, ((0, 0), (CONV_WIDTH - 1, 0), (0, 0)))
    y = conv_b
    for j in range(CONV_WIDTH):
        y = y + conv_w[j] * hp[:, j:j + S, :]
    a, g = jnp.split(y, 2, axis=-1)
    return (jax.nn.silu(g) * a) @ w_down

def setup_inputs(seed: int = 0) -> dict:
    key = jax.random.key(seed)
    ks = jax.random.split(key, 20)
    f32 = jnp.float32
    x = jax.random.normal(ks[0], (BATCH, SEQ, D_MODEL), f32)
    c = jax.random.normal(ks[1], (BATCH, D_MODEL), f32)
    positions = (jax.random.randint(ks[2], (BATCH, 1), 0, MAX_POS_OFFSET)
                 + jnp.arange(SEQ)[None, :]).astype(jnp.int32)
    w_ada = jax.random.normal(ks[3], (DEPTH, D_MODEL, 6 * D_MODEL), f32) * ADA_STD
    b_ada = jax.random.normal(ks[4], (DEPTH, 6 * D_MODEL), f32) * 0.01
    col_scale = jnp.concatenate([jnp.full((n,), DEEPNORM_BETA if is_v else 1.0, f32)
                                 for n, is_v in zip(IN_SIZES, IN_IS_VALUE)])
    w_in = jax.random.normal(ks[5], (DEPTH, D_MODEL, IN_COLS), f32) * (D_MODEL ** -0.5) * col_scale
    w_gla_gate = jax.random.normal(ks[6], (DEPTH, GLA_GATE_RANK, GLA_HEADS * GLA_DK), f32) * (GLA_GATE_RANK ** -0.5)
    b_gla_gate = jax.random.normal(ks[7], (DEPTH, GLA_HEADS * GLA_DK), f32) * 0.1
    gla_norm_g = 1.0 + 0.02 * jax.random.normal(ks[8], (DEPTH, GLA_DV), f32)
    w_out = jax.random.normal(ks[9], (DEPTH, D_MODEL, D_MODEL), f32) * (D_MODEL ** -0.5) * DEEPNORM_BETA
    ln1_g = 1.0 + 0.02 * jax.random.normal(ks[10], (DEPTH, D_MODEL), f32)
    ln1_b = 0.02 * jax.random.normal(ks[11], (DEPTH, D_MODEL), f32)
    w_up = jax.random.normal(ks[12], (DEPTH, D_MODEL, 2 * D_FF), f32) * (D_MODEL ** -0.5) * DEEPNORM_BETA
    conv_w = jax.random.normal(ks[13], (DEPTH, CONV_WIDTH, 2 * D_FF), f32) * (CONV_WIDTH ** -0.5)
    conv_b = 0.01 * jax.random.normal(ks[14], (DEPTH, 2 * D_FF), f32)
    w_down = jax.random.normal(ks[15], (DEPTH, D_FF, D_MODEL), f32) * (D_FF ** -0.5) * DEEPNORM_BETA
    ln2_g = 1.0 + 0.02 * jax.random.normal(ks[16], (DEPTH, D_MODEL), f32)
    ln2_b = 0.02 * jax.random.normal(ks[17], (DEPTH, D_MODEL), f32)
    return {"x": x, "c": c, "positions": positions, "w_ada": w_ada, "b_ada": b_ada,
            "w_in": w_in, "w_gla_gate": w_gla_gate, "b_gla_gate": b_gla_gate,
            "gla_norm_g": gla_norm_g, "w_out": w_out, "ln1_g": ln1_g, "ln1_b": ln1_b,
            "w_up": w_up, "conv_w": conv_w, "conv_b": conv_b, "w_down": w_down,
            "ln2_g": ln2_g, "ln2_b": ln2_b}

def reference(x, c, positions, w_ada, b_ada, w_in, w_gla_gate, b_gla_gate, gla_norm_g, w_out,
              ln1_g, ln1_b, w_up, conv_w, conv_b, w_down, ln2_g, ln2_b):
    for layer in range(DEPTH):
        mod = jax.nn.silu(c) @ w_ada[layer] + b_ada[layer]
        sh1, sc1, g1, sh2, sc2, g2 = [m[:, None, :] for m in jnp.split(mod, 6, axis=-1)]
        u = x * (1.0 + sc1) + sh1
        y = token_mixer(u, positions, w_in[layer], w_gla_gate[layer], b_gla_gate[layer],
                        gla_norm_g[layer], w_out[layer])
        x = layer_norm(DEEPNORM_ALPHA * x + (1.0 + g1) * y, ln1_g[layer], ln1_b[layer])
        u = x * (1.0 + sc2) + sh2
        y = conv_ffn(u, w_up[layer], conv_w[layer], conv_b[layer], w_down[layer])
        x = layer_norm(DEEPNORM_ALPHA * x + (1.0 + g2) * y, ln2_g[layer], ln2_b[layer])
    return x


_drawn_inputs = setup_inputs


def setup_inputs(seed=0):
    import zlib

    import numpy as np

    out = dict(_drawn_inputs(seed))
    spreads = {}
    factors = {'b_ada': 7.301,
     'b_gla_gate': 5.992,
     'gla_norm_g': 25.746,
     'ln1_g': 7.78,
     'ln1_b': 7.942,
     'conv_b': 26.383,
     'ln2_g': 24.467,
     'ln2_b': 23.777}
    for name, (base, spread) in spreads.items():
        noise = np.random.default_rng([zlib.crc32(name.encode()), seed]).standard_normal(out[name].shape)
        drawn = base * np.exp(spread * noise) if base else spread * noise
        out[name] = __import__('jax').numpy.asarray(drawn.astype(out[name].dtype))
    for name, factor in factors.items():
        out[name] = (out[name] * factor).astype(out[name].dtype)
    return out
```

```python
import math

import numpy as np

import concourse.bass as bass
from concourse import mybir
from concourse.alu_op_type import AluOpType as ALU

ACT = mybir.ActivationFunctionType
F32 = mybir.dt.float32
F32R = mybir.dt.float32r
I32 = mybir.dt.int32
AX_X = mybir.AxisListType.X

P = 128
D = 2048
T = 512
KT = D // P
TT = T // P
DFF = 5632
FT = DFF // P
GROUPS = 8
GLA = 4
GW = D // GROUPS
RANK = 16
TAU = 16.0
SCALE = 128.0 ** -0.5
ALPHA = 2.0 ** 0.25
LN_EPS, RMS_EPS = 1e-5, 1e-6
WBLK = 2048
LEVELS = 7
SETS = LEVELS + 2
FIRST_W = 6 * P + RANK
PRO = KT // 2
FFN0 = PRO + 8 * GROUPS - 6
PAIRS = 4
FG = FT // PAIRS
NBLK = FFN0 + FG * 12
ADA_SLOTS = 4
SHIFT1, SCALE1, GATE1, SHIFT2, SCALE2, GATE2 = range(0, 96, 16)

V_BADA, V_LN1G, V_LN1B, V_LN2G, V_LN2B = 0, 96, 112, 128, 144
V_GNORM, V_INVF, V_SGN, V_EPS, V_CONV = 160, 162, 163, 164, 168
NVEC = V_CONV + FT * 8

FIRST_LAYOUT = [("p", b) for b in range(6)]
LAYOUT = [("p", 0), ("o", 0), ("o", 1)] + [("p", b) for b in range(1, 6)]
GLA_AT, SQ_AT, MS_AT, O_AT = 3, 20, 22, 23
S_AT = {3 * k + 3: k for k in range(8)}
T_AT = {3 * k + 5: k for k in range(8)}
A_AT = {3 * k + 7: k for k in range(8)}
PAIR_AT = 29
FILL_AT = 2
ADA_FIRST_AT = list(range(16)) + [u for u in range(16, 24) for _ in range(2)]
ADA_AT = [u for u in range(12, 32) if u % 5]


def build(nc, x, c_rows, pos_rows, w_first, w_stream, w_ada_t, w_gate, vec, decay_sums, level_masks,
          band_bias, eye, out):
    used = [nc.sbuf_base + 31 - (nc.sbuf_base + 31) % 32]

    def sb(name, shape, dt, at=None):
        size = int(np.prod(shape[1:])) * 4
        if at is None:
            at = used[0]
            used[0] += (size + 31) // 32 * 32
            assert used[0] <= nc.sbuf_usable_end, (name, used[0])
        tile = nc.alloc_sbuf_tensor_at(name, shape, dt, offset=at)
        where[name] = at
        return tile

    where = {}
    res = sb("res", [P, KT, T], F32)
    uH = sb("uH", [P, KT, T], F32R)
    uL = sb("uL", [P, KT, T], F32R)
    raw = [sb(f"raw{s}", [P, WBLK], F32) for s in range(2)]
    wH = [sb(f"wH{s}", [P, WBLK], F32R) for s in range(2)]
    wL = [sb(f"wL{s}", [P, WBLK], F32R) for s in range(2)]
    ada_half = [sb("ada_half0", [P, WBLK // 2], F32)]
    csil = sb("csil", [P, D], F32)
    vecs = sb("vecs", [P, NVEC], F32)
    mod = sb("mod", [P, 96], F32)
    mod1 = sb("mod1", [P, 3, KT], F32)
    acc = sb("acc", [P, 32], F32)
    acc16 = sb("acc16", [P, 16], F32)
    lnA = sb("lnA", [P, 4, KT], F32)
    ident = sb("ident", [P, P], F32)
    ones_rms = sb("ones_rms", [P, P], F32)
    ones_ln = sb("ones_ln", [P, P], F32)
    mixer0 = used[0]
    stage = sb("stage", [P, 4, T], F32)
    Vw = sb("Vw", [P, TT, GW], F32)
    oH = sb("oH", [P, 2, T], F32R)
    oL = sb("oL", [P, 2, T], F32R)
    dsum = sb("dsum", [P, SETS, P], F32)
    masks = sb("masks", [P, LEVELS + 1, P], F32)
    cosT = sb("cosT", [P, T], F32)
    sinT = sb("sinT", [P, T], F32)
    bias = sb("bias", [P, T], F32)
    work0 = used[0]
    glr = sb("glr", [RANK + 1, T], F32)
    wgate = sb("wgate", [RANK + 1, P], F32)
    la = sb("la", [P, TT, P], F32)
    qw = sb("qw", [P, T], F32)
    kw = sb("kw", [P, T], F32)
    sg = sb("sg", [P, 2, T], F32)
    KE = sb("KE", [P, SETS, P], F32)
    Q = sb("Q", [P, SETS, P], F32)
    ssum = sb("ssum", [P, P], F32)
    state = sb("state", [P, GW], F32)
    khT = sb("khT", [P, P], F32)
    o = sb("o", [P, 2, T], F32)
    absz = sb("absz", [P, T], F32, at=where["Q"])
    softp = sb("softp", [P, T], F32, at=where["Q"] + T * 4)
    osq = sb("osq", [P, 2, T], F32, at=where["Q"])
    rms = sb("rms", [P, T], F32, at=where["KE"])
    def over(name, shape, dt, off):
        assert work0 + off + int(np.prod(shape[1:])) * 4 <= used[0], name
        return sb(name, shape, dt, at=work0 + off)
    rot = over("rot", [P, 4, T], F32, 2048)
    rtmp = over("rtmp", [P, 2, T], F32, 10240)
    Pm = over("Pm", [P, 2, T], F32, 14336)
    PT = over("PT", [P, 2, T], F32, 18432)
    astat = over("astat", [P, 2, 4], F32, 22528)
    ring_u = [over(f"ring_u{s}", [P, T], F32, 2560 + s * 2048) for s in range(4)]
    ada_big = [sb("ada_big0", [P, WBLK], F32, at=where["stage"]),
               sb("ada_big1", [P, WBLK], F32, at=where["Vw"])]
    ada_big += [over(f"ada_big{s}", [P, WBLK], F32, 10752 + (s - 2) * WBLK * 4) for s in (2, 3)]
    assert where["oL"] >= where["Vw"] + WBLK * 4
    posi = sb("posi", [P, T], I32, at=where["cosT"])
    ang = sb("ang", [P, T], F32, at=where["oL"])
    turns = sb("turns", [P, T], F32, at=where["oL"] + T * 4)
    ada_half.append(sb("ada_half1", [P, WBLK // 2], F32, at=where["oL"]))
    sofar = used[0]
    used[0] = mixer0
    vH = sb("vH", [P, PAIRS, T], F32R)
    vL = sb("vL", [P, PAIRS, T], F32R)
    yv = sb("yv", [P, 2, T], F32)
    yg = sb("yg", [P, 2, T], F32)
    sgate = sb("sgate", [P, 2, T], F32)
    prod = sb("prod", [P, 2, T], F32)
    ring_n = [sb(f"ring_n{s}", [P, T], F32) for s in range(4)]
    rstd = sb("rstd", [P, T], F32)
    zsum = sb("zsum", [P, T], F32)
    used[0] = max(used[0], sofar)

    ps = nc.alloc_psum_tensor("ps", [P, 8, T], F32)

    names = """const_in pos_in gla_const_in att_const_in wgate_in out_done
        w_hi w_lo silu_c ada_dot ada_half_dot mod_step
        uf_ready uh_ready ul_ready ax_ready first_used first_done
        proj_done proj_evac glr_ready glr_ones wout_done y_added
        logit_done abs_ready nexp_ready softp_ready la_ready gla_qk
        dsum_done exp_ready qk_scaled score_done masked ssum_ready
        kt_done kht_ready upd_done state_ready gla_o_done o_evac
        gate_ready sq_ready ms_done rt_ready rstd_ready o_step oh_ready ol_ready
        pos_step rot_step s_done biased neg_ready p_exp p_step tr_done pt_ready ao_done
        zsum_step sum_done cz_ready csq_ready var_done sd_ready lnr_ready ln_vec
        n_ready u2h_ready u2l_ready
        up_done base_ready conv_step sil_ready pr_ready vh_ready vl_ready down_done z2_step z2_added
        fin_ready""".split()
    S = {n: nc.alloc_semaphore(n) for n in names}
    ada_big_in = [nc.alloc_semaphore(f"ada_big{s}_in") for s in range(ADA_SLOTS)]
    ada_half_in = [nc.alloc_semaphore(f"ada_half{s}_in") for s in range(2)]
    x_in = [nc.alloc_semaphore(f"x{q}_in") for q in range(4)]
    raw_in = [nc.alloc_semaphore(f"raw{s}_in") for s in range(2)]

    def three(bank, wh, wl, ah, al, first, last):
        nc.tensor.matmul(bank, wh, ah, start=first, stop=False, skip_group_check=True)
        nc.tensor.matmul(bank, wh, al, start=False, stop=False, skip_group_check=True)
        return nc.tensor.matmul(bank, wl, ah, start=False, stop=last, skip_group_check=True)

    with nc.Block() as block:
        @block.sync
        def _(sp):
            def load_raw(n, n_const, slot):
                sp.wait_ge(S["w_lo"], n + (n_const - 1))
                sp.dma_start(raw[slot][:], w_stream[n + (n_const - PRO)]).then_inc(raw_in[slot], 16)

            sp.dma_start(csil[:], c_rows).then_inc(S["const_in"], 16)
            sp.dma_start(vecs[:], vec).then_inc(S["const_in"], 16)
            for k in range(KT):
                for i, part in enumerate((SHIFT1, SCALE1)):
                    m = 2 * k + i
                    if m >= ADA_SLOTS:
                        sp.wait_ge(S["ada_dot"], m + 1 - ADA_SLOTS)
                    sp.dma_start(ada_big[m % ADA_SLOTS][:], w_ada_t[part + k])\
                        .then_inc(ada_big_in[m % ADA_SLOTS], 16)
                if k % 4 == 0:
                    sp.dma_start(res[:, k:k + 4, :], x[:, k:k + 4, :]).then_inc(x_in[k // 4], 16)
                if k % 2 == 0:
                    n = k // 2
                    if n >= 2:
                        sp.wait_ge(S["w_lo"], n - 1)
                    sp.dma_start(raw[n % 2][:, 0:2 * FIRST_W], w_first[n]).then_inc(raw_in[n % 2], 16)
                if k == 8:
                    sp.dma_start(posi[:], pos_rows).then_inc(S["pos_in"], 16)
            load_raw(PRO, 0, 0)
            sp.dma_start(wgate[:], w_gate[0]).then_inc(S["wgate_in"], 16)
            sp.dma_start(dsum[:], decay_sums).then_inc(S["gla_const_in"], 16)
            sp.dma_start(masks[:], level_masks).then_inc(S["gla_const_in"], 16)
            sp.dma_start(ident[:], eye[:, 0, :]).then_inc(S["gla_const_in"], 16)
            sp.dma_start(ones_rms[:], eye[:, 1, :]).then_inc(S["gla_const_in"], 16)
            load_raw(PRO, 1, 1)
            load_raw(PRO, 2, 0)
            load_raw(PRO, 3, 1)
            sp.dma_start(bias[:], band_bias).then_inc(S["att_const_in"], 16)
            sp.dma_start(ones_ln[:], eye[:, 2, :]).then_inc(S["att_const_in"], 16)

            sp.wait_ge(S["pos_step"], 13)
            for i in range(-1, 6):
                for h, u in enumerate(ADA_FIRST_AT):
                    if u // 4 == i + 1:
                        if h >= 2:
                            sp.wait_ge(S["ada_half_dot"], h - 1)
                        sp.dma_start(ada_half[h % 2][:], w_ada_t[GATE1 + h // 2][:, h % 2 * 1024:(h % 2 + 1) * 1024])\
                            .then_inc(ada_half_in[h % 2], 16)
                if i >= 0:
                    load_raw(PRO, i + 4, i % 2)

            def window(w):
                for i in range(8):
                    for h, u in enumerate(ADA_AT):
                        if u // 4 == i + 1:
                            sp.wait_ge(S["ada_half_dot"], 16 * w + (16 + h))
                            sp.dma_start(ada_half[0][:], w_ada_t[w * 8 + (SHIFT2 - 8 + h // 2)]
                                         [:, h % 2 * 1024:(h % 2 + 1) * 1024]).then_inc(ada_half_in[0], 16)
                    load_raw(8 * w, 10 + i, i % 2)

            def gate_weights(w):
                sp.wait_ge(S["logit_done"], w)
                sp.dma_start(wgate[:], w_gate[w]).then_inc(S["wgate_in"], 16)

            with sp.Fori(1, GLA) as w:
                gate_weights(w)
                window(w)
            with sp.Fori(GLA, GROUPS - 1) as w:
                window(w)
            with sp.Fori(FFN0, NBLK - 1, 2) as n:
                load_raw(n, 0, 0)
                load_raw(n, 1, 1)
            for k in range(KT):
                sp.wait_ge(S["fin_ready"], k + 1)
                sp.dma_start(out[:, k, :], res[:, k, :]).then_inc(S["out_done"], 16)
            sp.wait_ge(S["out_done"], 16 * KT)

        @block.gpsimd
        def _(pool):
            def low(n, s, size=WBLK):
                pool.wait_ge(S["w_hi"], n + 1)
                nc.gpsimd.tensor_tensor(wL[s][:, 0:size], raw[s][:, 0:size], wH[s][:, 0:size].bitcast(F32),
                                        ALU.subtract).then_inc(S["w_lo"], 1)

            def add_tile(j, f, source, count):
                pool.wait_ge(source, count + f + 1)
                if f == 1:
                    first = res[:, 0, :]
                else:
                    pool.wait_ge(S["zsum_step"], (KT - 1) * j + f - 1)
                    first = zsum[:]
                nc.gpsimd.tensor_tensor(zsum[:], first, res[:, f, :], ALU.add).then_inc(S["zsum_step"], 1)

            with pool.Fori(0, PRO - 1, 2) as n:
                low(n, 0, 2 * FIRST_W)
                low(n + 1, 1, 2 * FIRST_W)
            with pool.Fori(PRO, FFN0 - 1, 2) as n:
                low(n, 0)
                low(n + 1, 1)
            for d in range(2):
                for f in range(max(1, 8 * d), 8 * d + 8):
                    add_tile(0, f, S["y_added"], 16 * (GROUPS - 1))
                low(FFN0 + d, d)
            with pool.Fori(FFN0 + 2, NBLK - 1, 2) as n:
                low(n, 0)
                low(n + 1, 1)
            for f in range(1, KT):
                add_tile(1, f, S["z2_added"], 16 * FG)

        @block.scalar
        def _(act):
            def high(s, landed, freed=None, count=None, size=WBLK):
                act.wait_ge(raw_in[s], landed)
                if freed is not None:
                    act.wait_ge(freed, count)
                nc.scalar.activation(wH[s][:, 0:size], raw[s][:, 0:size], ACT.Copy).then_inc(S["w_hi"], 1)

            def landed(n):
                return 16 * (n // 2 + 1)

            def high_in_window(w, i, layout):
                kind, b = layout[i]
                at = landed(PRO + 2 + i) if layout is FIRST_LAYOUT else 64 * w + landed(8 + i)
                if kind == "p":
                    high(i % 2, at, S["proj_done"], 6 * w + (b + 1))
                else:
                    high(i % 2, at, S["wout_done"], 16 * w + (8 * b - 8))

            def evac(w, b, bank=None):
                if b < 4:
                    bank = b % 2 if bank is None else bank
                    nc.scalar.activation(stage[:, b, :], ps[:, bank, :], ACT.Copy)\
                        .then_inc(S["proj_evac"], 1)
                else:
                    nc.scalar.activation(Vw[:].rearrange("p t v -> p (t v)"),
                                         ps[:, 2:4, :].rearrange("p b v -> p (b v)"), ACT.Copy)\
                        .then_inc(S["proj_evac"], 1)

            def evac_in_window(w, b, free):
                act.wait_ge(S["proj_done"], 6 * w + ((b if b < 4 else 5) + 1))
                if free is not None:
                    act.wait_ge(*free)
                evac(w, b)

            act.wait_ge(S["const_in"], 32)
            nc.scalar.activation(csil[:], csil[:], ACT.Silu).then_inc(S["silu_c"], 1)
            high(0, landed(0), size=2 * FIRST_W)
            high(1, landed(1), size=2 * FIRST_W)
            for k in range(KT):
                act.wait_ge(S["uf_ready"], k + 1)
                nc.scalar.activation(uH[:, k, :], ring_u[k % 4][:], ACT.Identity, bias=mod[:, k:k + 1])\
                    .then_inc(S["uh_ready"], 1)
                nc.scalar.activation(res[:, k, :], res[:, k, :], ACT.Copy, scale=ALPHA)\
                    .then_inc(S["ax_ready"], 1)
                if k >= 2 and k % 2 == 0:
                    n = k // 2 + 1
                    high(n % 2, landed(n), S["first_used"], n - 1, 2 * FIRST_W if n < PRO else WBLK)
                if k == 11:
                    act.wait_ge(S["pos_step"], 10)
                    nc.scalar.activation(sinT[:], ang[:], ACT.Sin).then_inc(S["rt_ready"], 1)
                    nc.scalar.activation(cosT[:], ang[:], ACT.Sin, scale=0.5).then_inc(S["rt_ready"], 1)
            act.wait_ge(S["first_done"], 1)
            evac(-1, 0, 0)
            act.wait_ge(S["first_done"], 2)
            evac(-1, 1, 1)
            act.wait_ge(S["first_done"], 3)
            act.wait_ge(S["glr_ones"], 1)
            nc.scalar.activation(glr[0:RANK, :], ps[0:RANK, 7, :], ACT.Copy).then_inc(S["glr_ready"], 1)
            act.wait_ge(S["first_done"], 5)
            evac(-1, 2, 4)
            act.wait_ge(S["first_done"], 6)
            evac(-1, 3, 5)
            high(1, landed(PRO + 1), S["first_done"], 6)
            evac(-1, 4)

            def gla_window(w, layout):
                units = 4 * len(layout)
                for u in range(units):
                    if u == 1:
                        act.wait_ge(S["logit_done"], w + 1)
                        nc.scalar.activation(absz[:], ps[:, 4, :], ACT.Abs).then_inc(S["abs_ready"], 1)
                        act.wait_ge(S["abs_ready"], w + 1)
                        nc.scalar.activation(softp[:], absz[:], ACT.Exp, scale=-1.0).then_inc(S["nexp_ready"], 1)
                        act.wait_ge(S["nexp_ready"], w + 1)
                        nc.scalar.activation(absz[:], softp[:], ACT.Ln, bias=vecs[:, V_EPS + 2:V_EPS + 3])\
                            .then_inc(S["softp_ready"], 1)
                    c, step = (u - GLA_AT) // 4, (u - GLA_AT) % 4
                    cc = 4 * w + c
                    if 0 <= c < 4:
                        if step == 0:
                            for j in range(2):
                                act.wait_ge(S["dsum_done"], 3 * cc + j + 1)
                                if c > 0:
                                    act.wait_ge(S["score_done"], 3 * cc + (j - 2))
                                elif j == 0:
                                    act.wait_ge(S["la_ready"], w + 1)
                                nc.scalar.activation(KE[:, 3 * j:3 * j + 3, :].rearrange("p s t -> p (s t)"),
                                                     ps[:, 4 + j, 0:3 * P], ACT.Exp).then_inc(S["exp_ready"], 1)
                        if step == 1:
                            act.wait_ge(S["dsum_done"], 3 * cc + 3)
                            if c > 0:
                                act.wait_ge(S["score_done"], 3 * cc)
                                act.wait_ge(S["kt_done"], 3 * w + c)
                                if c > 1:
                                    act.wait_ge(S["state_ready"], 3 * w + c)
                            nc.scalar.activation(KE[:, 6:9, :].rearrange("p s t -> p (s t)"),
                                                 ps[:, 4, 0:3 * P], ACT.Exp).then_inc(S["exp_ready"], 1)
                        if step == 3 and c < 3:
                            act.wait_ge(S["kt_done"], 3 * w + c + 1)
                            if c > 0:
                                act.wait_ge(S["upd_done"], 3 * w + c)
                            nc.scalar.activation(khT[:], ps[:, 3, 0:P], ACT.Copy).then_inc(S["kht_ready"], 1)
                    if step == 0 and 1 <= c <= 4:
                        act.wait_ge(S["gla_o_done"], 4 * w + c)
                        nc.scalar.activation(o[:, :, (c - 1) * P:c * P],
                                             ps[:, 7, 0:GW].rearrange("p (d t) -> p d t", d=2),
                                             ACT.Copy).then_inc(S["o_evac"], 1)
                    if u == 10:
                        nc.scalar.activation(sg[:].rearrange("p d t -> p (d t)"),
                                             stage[:, 2:4, :].rearrange("p d t -> p (d t)"), ACT.Silu)\
                            .then_inc(S["gate_ready"], 1)
                    if u == SQ_AT:
                        act.wait_ge(S["o_evac"], 4 * w + 4)
                        act.wait_ge(S["ssum_ready"], 4 * w + 4)
                        nc.scalar.activation(osq[:], o[:], ACT.Square).then_inc(S["sq_ready"], 1)
                    if u == MS_AT:
                        act.wait_ge(S["ms_done"], w + 1)
                        nc.scalar.activation(rms[:], ps[:, 6, :], ACT.Sqrt, bias=vecs[:, V_EPS:V_EPS + 1])\
                            .then_inc(S["rt_ready"], 1)
                    if u == O_AT:
                        act.wait_ge(S["o_step"], 3 * w + 3)
                        nc.scalar.activation(oH[:], o[:], ACT.Copy).then_inc(S["oh_ready"], 1)
                    if u % 4 == 3:
                        i = u // 4
                        high_in_window(w, i, layout)
                        kind, b = layout[i]
                        if kind == "p" and b < 4:
                            evac_in_window(w, b, (S["gla_qk"], 2 * w + 2) if b < 2
                                           else (S["gate_ready"], w + 1))
                        elif kind == "p" and b == 5:
                            evac_in_window(w, 4, None)

            gla_window(0, FIRST_LAYOUT)
            with act.Fori(1, GLA) as w:
                gla_window(w, LAYOUT)

            def att_window(w, last):
                v = w - GLA
                for u in range(32):
                    if u in S_AT:
                        k = S_AT[u]
                        act.wait_ge(S["neg_ready"], 8 * v + k + 1)
                        nt = (k % 4 + 1) * P
                        nc.scalar.activation(Pm[:, k % 2, 0:nt], Pm[:, k % 2, 0:nt], ACT.Exp,
                                             bias=astat[:, k % 2, 0:1], accum_out=astat[:, k % 2, 1:2])\
                            .then_inc(S["p_exp"], 1)
                    if u in T_AT:
                        k = T_AT[u]
                        act.wait_ge(S["tr_done"], 8 * v + k + 1)
                        if k >= 2:
                            act.wait_ge(S["ao_done"], 8 * v + k - 1)
                        nt = (k % 4 + 1) * P
                        nc.scalar.activation(PT[:, k % 2, 0:nt], ps[:, 6 + k % 2, 0:nt], ACT.Copy)\
                            .then_inc(S["pt_ready"], 1)
                    if u in A_AT:
                        k = A_AT[u]
                        act.wait_ge(S["ao_done"], 8 * v + k + 1)
                        if k == 0:
                            act.wait_ge(S["ol_ready"], w)
                        nc.scalar.activation(o[:, k // 4, k % 4 * P:(k % 4 + 1) * P],
                                             ps[:, 4 + k % 2, 0:P], ACT.Copy).then_inc(S["o_evac"], 1)
                    if u == PAIR_AT:
                        act.wait_ge(S["o_evac"], 16 + 8 * v + 8)
                        if last:
                            act.wait_ge(S["wout_done"], 16 * w)
                        nc.scalar.activation(oH[:], o[:], ACT.Copy).then_inc(S["oh_ready"], 1)
                    if last:
                        if u in (FILL_AT + 7, FILL_AT + 15):
                            d = (u - FILL_AT) // 8
                            high(d, landed(FFN0 - 2 + d), S["wout_done"], 16 * (w - 1) + 8 * (d + 1))
                    elif u % 4 == 3:
                        i = u // 4
                        high_in_window(w, i, LAYOUT)
                        kind, b = LAYOUT[i]
                        if kind == "p" and b < 4:
                            evac_in_window(w, b, (S["rot_step"], 16 * v + 4 * b + 4))
                        elif kind == "p" and b == 5:
                            evac_in_window(w, 4, None)

            with act.Fori(GLA, GROUPS - 1) as w:
                att_window(w, False)
            att_window(GROUPS - 1, True)
            for d in range(2):
                high(d, landed(FFN0 + d), S["wout_done"], 16 * (GROUPS - 1) + 8 * (d + 1))

            def norm_steps(j):
                for k in range(KT):
                    act.wait_ge(S["cz_ready"], KT * j + k + 1)
                    if k >= 4:
                        act.wait_ge(S["var_done"], KT * j + k - 3)
                    nc.scalar.activation(ring_n[k % 4][:], res[:, k, :], ACT.Square)\
                        .then_inc(S["csq_ready"], 1)
                act.wait_ge(S["var_done"], KT * (j + 1))
                nc.scalar.activation(rstd[:], ps[:, (5, 1)[j], :], ACT.Sqrt, bias=vecs[:, V_EPS + 1:V_EPS + 2])\
                    .then_inc(S["sd_ready"], 1)

            norm_steps(0)
            for k in range(KT):
                act.wait_ge(S["n_ready"], k + 1)
                nc.scalar.activation(uH[:, k, :], ring_n[k % 4][:], ACT.Identity,
                                     bias=lnA[:, 1, k:k + 1]).then_inc(S["u2h_ready"], 1)

            def high_at(g, i):
                m = FFN0 - 2 + i
                if i < 2 or i > 5:
                    freed, count = S["up_done"], 8 * g + ((i if i < 2 else i - 4) + 1)
                else:
                    freed, count = S["down_done"], 16 * g + (4 * (i - 1) - 16)
                high(m % 2, 96 * g + 16 * (m // 2 + 1), freed, count)

            def conv_column(g, p, i, tap):
                return vecs[:, bass.ds(g * 32 + (V_CONV + 8 * p + 4 * i + tap), 1)]

            def base_steps(g, p, make_high):
                q = 4 * g + p
                for i in range(2):
                    make_high(i)
                    act.wait_ge(S["up_done"], 2 * q + (i + 1))
                    if p >= 2 or not isinstance(g, int):
                        act.wait_ge(S["pr_ready"], q - 1)
                    nc.scalar.activation((yv, yg)[i][:, p % 2, :], ps[:, 2 * (p % 2) + i, :], ACT.Identity,
                                         scale=conv_column(g, p, i, 2), bias=conv_column(g, p, i, 3))\
                        .then_inc(S["base_ready"], 1)
                act.wait_ge(S["conv_step"], 4 * q + 4)
                nc.scalar.activation(sgate[:, p % 2, :], yg[:, p % 2, :], ACT.Silu)\
                    .then_inc(S["sil_ready"], 1)

            def v_high(g, p):
                act.wait_ge(S["pr_ready"], 4 * g + (p + 1))
                nc.scalar.activation(vH[:, p, :], prod[:, p % 2, :], ACT.Copy).then_inc(S["vh_ready"], 1)

            for p in range(PAIRS):
                base_steps(0, p, lambda i: high((FFN0 + 2 * p + i) % 2, landed(FFN0 + 2 * p + i + 2),
                                                S["up_done"], 2 * p + i + 1))
                v_high(0, p)
            with act.Fori(1, FG) as g:
                base_steps(g, 0, lambda i: high_at(g, i))
                for d in range(4):
                    high_at(g, 2 + d)
                v_high(g, 0)
                for p in range(1, PAIRS):
                    base_steps(g, p, lambda i: high_at(g, 4 + 2 * p + i))
                    v_high(g, p)
            for d in range(2):
                high((NBLK - 2 + d) % 2, landed(NBLK - 2 + d), S["down_done"], 16 * (FG - 1) + 4 * (d + 1))
            norm_steps(1)
            for k in range(KT):
                act.wait_ge(S["n_ready"], KT + k + 1)
                nc.scalar.activation(res[:, k, :], res[:, k, :], ACT.Identity,
                                     bias=vecs[:, V_LN2B + k:V_LN2B + k + 1]).then_inc(S["fin_ready"], 1)

        @block.vector
        def _(dve):
            V = nc.vector

            def u_low(k):
                dve.wait_ge(S["uh_ready"], k + 1)
                V.scalar_tensor_tensor(out=uL[:, k, :], in0=ring_u[k % 4][:], scalar=mod[:, k:k + 1],
                                       in1=uH[:, k, :].bitcast(F32), op0=ALU.add, op1=ALU.subtract)\
                    .then_inc(S["ul_ready"], 1)

            chain = [0]

            def pos(ins):
                chain[0] += 1
                ins.then_inc(S["pos_step"], 1)
                dve.wait_ge(S["pos_step"], chain[0])

            BIG = 1.5 * 2.0 ** 23
            TWO_PI = 2.0 * math.pi
            C1 = 6.28125
            C2 = float(np.float32(math.floor((TWO_PI - C1) * 2.0 ** 20) / 2.0 ** 20))
            C3 = float(np.float32(TWO_PI - C1 - C2))

            def angles():
                dve.wait_ge(S["pos_in"], 16)
                pos(V.tensor_copy(ang[:], posi[:]))
                pos(V.tensor_scalar(ang[:], ang[:], vecs[:, V_INVF:V_INVF + 1], None, ALU.mult))
                pos(V.tensor_scalar(turns[:], ang[:], 1.0 / TWO_PI, None, ALU.mult))
                pos(V.tensor_scalar(turns[:], turns[:], BIG, None, ALU.add))
                pos(V.tensor_scalar(turns[:], turns[:], -BIG, None, ALU.add))
                for c in (C1, C2, C3):
                    pos(V.scalar_tensor_tensor(out=ang[:], in0=turns[:], scalar=-c, in1=ang[:],
                                               op0=ALU.mult, op1=ALU.add))
                pos(V.tensor_scalar(ang[:], ang[:], math.pi, -math.pi, ALU.min, ALU.max))
                pos(V.tensor_scalar(ang[:], ang[:], 3.1415925, -3.1415925, ALU.min, ALU.max))

            def tables():
                dve.wait_ge(S["rt_ready"], 2)
                pos(V.tensor_scalar(sinT[:], sinT[:], vecs[:, V_SGN:V_SGN + 1], None, ALU.mult))
                pos(V.tensor_tensor(cosT[:], cosT[:], cosT[:], ALU.mult))
                pos(V.tensor_scalar(cosT[:], cosT[:], -2.0, 1.0, ALU.mult, ALU.add))

            dve.wait_ge(S["silu_c"], 1)
            for k in range(KT):
                for i in range(2):
                    m = 2 * k + i
                    s = m % ADA_SLOTS
                    dve.wait_ge(ada_big_in[s], 16 * (m // ADA_SLOTS + 1))
                    V.tensor_tensor_reduce(out=ada_big[s][:], in0=ada_big[s][:], in1=csil[:], scale=1.0,
                                           scalar=0.0, op0=ALU.mult, op1=ALU.add,
                                           accum_out=mod[:, k + KT * i:k + KT * i + 1])\
                        .then_inc(S["ada_dot"], 1)
                dve.wait_ge(S["ada_dot"], 2 * k + 2)
                V.tensor_tensor(mod[:, k:k + KT + 1:KT], mod[:, k:k + KT + 1:KT], vecs[:, k:k + KT + 1:KT],
                                ALU.add).then_inc(S["mod_step"], 1)
                if k > 0:
                    u_low(k - 1)
                dve.wait_ge(S["mod_step"], k + 1)
                dve.wait_ge(x_in[k // 4], 16)
                if k >= 4:
                    dve.wait_ge(S["ul_ready"], k - 3)
                V.scalar_tensor_tensor(out=ring_u[k % 4][:], in0=res[:, k, :], scalar=mod[:, KT + k:KT + k + 1],
                                       in1=res[:, k, :], op0=ALU.mult, op1=ALU.add)\
                    .then_inc(S["uf_ready"], 1)
                if k == 2:
                    V.memset(glr[:], 1.0).then_inc(S["glr_ones"], 1)
                if k == 10:
                    angles()
                if k == 12:
                    tables()
            u_low(KT - 1)

            def ada(w, i):
                slot = i % 2 if isinstance(w, int) else 0
                if isinstance(w, int):
                    dve.wait_ge(ada_half_in[slot], 16 * (i // 2 + 1))
                else:
                    dve.wait_ge(ada_half_in[0], 256 * w + 16 * (i + 1))
                V.tensor_tensor_reduce(out=ada_half[slot][:], in0=ada_half[slot][:],
                                       in1=csil[:, (i % 2) * 1024:(i % 2 + 1) * 1024], scale=1.0,
                                       scalar=0.0, op0=ALU.mult, op1=ALU.add,
                                       accum_out=acc[:, i:i + 1]).then_inc(S["ada_half_dot"], 1)

            def ada_end(w):
                n = 16 if isinstance(w, int) else 8
                dve.wait_ge(S["ada_half_dot"], 16 * w + 32)
                V.tensor_tensor(acc16[:, 0:n], acc[:, 0:2 * n:2], acc[:, 1:2 * n:2], ALU.add)\
                    .then_inc(S["mod_step"], 1)
                dve.wait_ge(S["mod_step"], 2 * w + (KT + 1))
                if isinstance(w, int):
                    V.scalar_tensor_tensor(out=mod1[:, 0, :], in0=acc16[:], scalar=1.0,
                                           in1=vecs[:, GATE1:GATE1 + KT], op0=ALU.add, op1=ALU.add)\
                        .then_inc(S["mod_step"], 1)
                else:
                    V.tensor_tensor(mod[:, bass.ds(w * 8 + (SHIFT2 - 8), 8)], acc16[:, 0:8],
                                    vecs[:, bass.ds(w * 8 + (SHIFT2 - 8), 8)], ALU.add)\
                        .then_inc(S["mod_step"], 1)
                dve.wait_ge(S["mod_step"], 2 * w + (KT + 2))

            def add_y(g, f):
                dve.wait_ge(S["wout_done"], 16 * g + f + 1)
                dve.wait_ge(S["y_added"], 16 * g)
                V.scalar_tensor_tensor(out=res[:, f, :], in0=ps[:, (f + 1) % 2, :], scalar=mod1[:, 0, f:f + 1],
                                       in1=res[:, f, :], op0=ALU.mult, op1=ALU.add)\
                    .then_inc(S["y_added"], 1)

            def in_unit(w, u, layout, ada_units):
                if layout[u // 4][0] == "o":
                    for f in (2 * (u - 4), 2 * (u - 4) + 1):
                        dve.wait_ge(S["wout_done"], 16 * w + (f - 15))
                        V.scalar_tensor_tensor(out=res[:, f, :], in0=ps[:, (f + 1) % 2, :],
                                               scalar=mod1[:, 0, f:f + 1], in1=res[:, f, :],
                                               op0=ALU.mult, op1=ALU.add).then_inc(S["y_added"], 1)
                for i, at in enumerate(ada_units):
                    if at == u:
                        ada(w, i)

            def gla_window(w, layout, ada_units):
                units = 4 * len(layout)
                for u in range(units):
                    if u == 0:
                        dve.wait_ge(S["proj_evac"], 5 * w + 2)
                        V.tensor_scalar(qw[:], stage[:, 0, :], SCALE, None, ALU.mult)\
                            .then_inc(S["gla_qk"], 1)
                        V.tensor_copy(kw[:], stage[:, 1, :]).then_inc(S["gla_qk"], 1)
                    if u == 2:
                        dve.wait_ge(S["softp_ready"], w + 1)
                        V.scalar_tensor_tensor(out=la[:].rearrange("p t f -> p (t f)"), in0=ps[:, 4, :],
                                               scalar=0.0, in1=absz[:], op0=ALU.min, op1=ALU.subtract)\
                            .then_inc(S["la_ready"], 1)
                        dve.wait_ge(S["la_ready"], w + 1)
                    c, step = (u - GLA_AT) // 4, (u - GLA_AT) % 4
                    cc = 4 * w + c
                    tok = slice(c * P, (c + 1) * P)

                    def scaled(j):
                        q_c, k_c = qw[:, tok], kw[:, tok]
                        dve.wait_ge(S["exp_ready"], 3 * cc + j + 1)
                        if j < 2:
                            sets = slice(3 * j, 3 * j + 3)
                            V.tensor_tensor(Q[:, sets, :], KE[:, sets, :],
                                            q_c.unsqueeze(1).to_broadcast([P, 3, P]), ALU.mult)\
                                .then_inc(S["qk_scaled"], 1)
                            kset = KE[:, sets, :]
                            n = 3
                        else:
                            if c > 0:
                                dve.wait_ge(S["gla_o_done"], cc)
                            V.tensor_tensor(Q[:, 6:9:2, :], KE[:, 6:8, :],
                                            q_c.unsqueeze(1).to_broadcast([P, 2, P]), ALU.mult)\
                                .then_inc(S["qk_scaled"], 1)
                            kset = KE[:, 6:9:2, :]
                            n = 2
                        dve.wait_ge(S["qk_scaled"], 6 * cc + 2 * j + 1)
                        V.tensor_tensor(kset, kset, k_c.unsqueeze(1).to_broadcast([P, n, P]), ALU.mult)\
                            .then_inc(S["qk_scaled"], 1)

                    def mask(j):
                        sets = slice(3 * j, min(3 * j + 3, 8))
                        n = 3 if j < 2 else 2
                        dve.wait_ge(S["score_done"], 3 * cc + j + 1)
                        V.tensor_tensor(Q[:, sets, :],
                                        ps[:, 6 + j % 2, 0:n * P].rearrange("p (s t) -> p s t", s=n),
                                        masks[:, sets, :], ALU.mult).then_inc(S["masked"], 1)

                    def state_step(c):
                        dve.wait_ge(S["upd_done"], 3 * w + c + 1)
                        if c == 0:
                            V.tensor_copy(state[:], ps[:, 2, 0:GW]).then_inc(S["state_ready"], 1)
                        else:
                            V.scalar_tensor_tensor(out=state[:], in0=state[:], scalar=KE[:, 7, P - 1:P],
                                                   in1=ps[:, 2, 0:GW], op0=ALU.mult, op1=ALU.add)\
                                .then_inc(S["state_ready"], 1)
                        dve.wait_ge(S["state_ready"], 3 * w + c + 1)

                    if 1 <= c <= 3 and step == 0:
                        dve.wait_ge(S["ssum_ready"], cc)
                        state_step(c - 1)
                    if 0 <= c < 4:
                        if step == 0:
                            scaled(0)
                            scaled(1)
                        elif step == 1:
                            scaled(2)
                            mask(0)
                        elif step == 2:
                            mask(1)
                        else:
                            mask(2)
                            dve.wait_ge(S["masked"], 3 * cc + 3)
                            if c > 0:
                                dve.wait_ge(S["gla_o_done"], cc)
                            V.tensor_reduce(out=ssum[:], in_=Q[:, 0:8, :].rearrange("p s t -> p t s"),
                                            op=ALU.add, axis=AX_X).then_inc(S["ssum_ready"], 1)
                    if u == MS_AT:
                        dve.wait_ge(S["rt_ready"], w + 3)
                        V.reciprocal(rms[:], rms[:]).then_inc(S["rstd_ready"], 1)
                        dve.wait_ge(S["rstd_ready"], w + 1)
                        V.tensor_tensor(o[:], o[:], rms[:].unsqueeze(1).to_broadcast([P, 2, T]), ALU.mult)\
                            .then_inc(S["o_step"], 1)
                        dve.wait_ge(S["o_step"], 3 * w + 1)
                        dve.wait_ge(S["gate_ready"], w + 1)
                        for d in range(2):
                            V.scalar_tensor_tensor(out=o[:, d, :], in0=o[:, d, :],
                                                   scalar=vecs[:, V_GNORM + d:V_GNORM + d + 1],
                                                   in1=sg[:, d, :], op0=ALU.mult, op1=ALU.mult)\
                                .then_inc(S["o_step"], 1)
                    if u == (units - 1 if layout is FIRST_LAYOUT else O_AT + 1):
                        if layout is FIRST_LAYOUT:
                            in_unit(w, u, layout, ada_units)
                            ada_end(w)
                        dve.wait_ge(S["oh_ready"], w + 1)
                        V.tensor_tensor(oL[:], o[:], oH[:].bitcast(F32), ALU.subtract)\
                            .then_inc(S["ol_ready"], 1)
                        if layout is FIRST_LAYOUT:
                            continue
                    in_unit(w, u, layout, ada_units)
                if layout is LAYOUT:
                    ada_end(w)

            gla_window(0, FIRST_LAYOUT, ADA_FIRST_AT)
            dve.wait_ge(S["ax_ready"], KT)
            with dve.Fori(1, GLA) as w:
                gla_window(w, LAYOUT, ADA_AT)

            def rotary(v, t):
                src, dst, tmp = stage[:, t, :], rot[:, t, :], rtmp[:, t % 2, :]
                s = SCALE if t % 2 == 0 else 1.0
                if t >= 2:
                    dve.wait_ge(S["rot_step"], 16 * v + 4 * (t - 1))
                V.scalar_tensor_tensor(out=dst, in0=src, scalar=s, in1=cosT[:], op0=ALU.mult,
                                       op1=ALU.mult).then_inc(S["rot_step"], 1)
                for lo, hi in ((0, 64), (64, 0)):
                    V.scalar_tensor_tensor(out=rtmp[lo:lo + 64, t % 2, :], in0=stage[hi:hi + 64, t, :],
                                           scalar=s, in1=sinT[hi:hi + 64, :], op0=ALU.mult,
                                           op1=ALU.mult).then_inc(S["rot_step"], 1)
                dve.wait_ge(S["rot_step"], 16 * v + 4 * t + 3)
                V.tensor_tensor(dst, dst, tmp, ALU.add).then_inc(S["rot_step"], 1)

            def att_window(w, last):
                v = w - GLA
                dve.wait_ge(S["proj_evac"], 5 * w + 4)
                for u in range(32):
                    if u == 0:
                        rotary(v, 0)
                        rotary(v, 1)
                    if u in (12, 13):
                        rotary(v, u - 10)
                    if u in S_AT:
                        k = S_AT[u]
                        nt = (k % 4 + 1) * P
                        dve.wait_ge(S["s_done"], 8 * v + k + 1)
                        if k >= 2:
                            dve.wait_ge(S["tr_done"], 8 * v + k - 1)
                            dve.wait_ge(S["p_step"], 16 * v + 2 * k - 2)
                        V.tensor_tensor(Pm[:, k % 2, 0:nt], ps[:, 4 + k % 2, 0:nt], bias[:, T - nt:T], ALU.add)\
                            .then_inc(S["biased"], 1)
                        dve.wait_ge(S["biased"], 8 * v + k + 1)
                        V.tensor_reduce(out=astat[:, k % 2, 0:1], in_=Pm[:, k % 2, 0:nt], op=ALU.max,
                                        axis=AX_X, negate=True).then_inc(S["neg_ready"], 1)
                    if last:
                        if FILL_AT <= u < FILL_AT + KT:
                            add_y(w - 1, u - FILL_AT)
                    else:
                        in_unit(w, u, LAYOUT, ADA_AT)
                    if u + 1 in T_AT:
                        k = T_AT[u + 1]
                        nt = (k % 4 + 1) * P
                        dve.wait_ge(S["p_exp"], 8 * v + k + 1)
                        V.reciprocal(astat[:, k % 2, 2:3], astat[:, k % 2, 1:2]).then_inc(S["p_step"], 1)
                        dve.wait_ge(S["p_step"], 16 * v + 2 * k + 1)
                        V.tensor_scalar(Pm[:, k % 2, 0:nt], Pm[:, k % 2, 0:nt], astat[:, k % 2, 2:3],
                                        None, ALU.mult).then_inc(S["p_step"], 1)
                    if u == PAIR_AT:
                        dve.wait_ge(S["oh_ready"], w + 1)
                        V.tensor_tensor(oL[:], o[:], oH[:].bitcast(F32), ALU.subtract)\
                            .then_inc(S["ol_ready"], 1)
                if not last:
                    ada_end(w)

            dve.wait_ge(S["att_const_in"], 32)
            with dve.Fori(GLA, GROUPS - 1) as w:
                att_window(w, False)
            V.tensor_scalar(mod1[:, 1, :], mod[:, SCALE2:SCALE2 + KT], 1.0, None, ALU.add)\
                .then_inc(S["ln_vec"], 1)
            V.tensor_scalar(mod1[:, 2, :], mod[:, GATE2:GATE2 + KT], 1.0, None, ALU.add)\
                .then_inc(S["ln_vec"], 1)
            dve.wait_ge(S["ln_vec"], 2)
            V.tensor_tensor(lnA[:, 0, :], vecs[:, V_LN1G:V_LN1G + KT], mod1[:, 1, :], ALU.mult)\
                .then_inc(S["ln_vec"], 1)
            V.tensor_tensor(lnA[:, 1, :], vecs[:, V_LN1B:V_LN1B + KT], mod1[:, 1, :], ALU.mult)\
                .then_inc(S["ln_vec"], 1)
            dve.wait_ge(S["ln_vec"], 4)
            V.tensor_tensor(lnA[:, 1, :], lnA[:, 1, :], mod[:, SHIFT2:SHIFT2 + KT], ALU.add)\
                .then_inc(S["ln_vec"], 1)
            V.tensor_scalar(lnA[:, 2, :], vecs[:, V_LN1G:V_LN1G + KT], ALPHA, None, ALU.mult)\
                .then_inc(S["ln_vec"], 1)
            V.tensor_scalar(lnA[:, 3, :], vecs[:, V_LN1B:V_LN1B + KT], ALPHA, None, ALU.mult)\
                .then_inc(S["ln_vec"], 1)
            dve.wait_ge(S["ln_vec"], 7)
            att_window(GROUPS - 1, True)
            for f in range(KT):
                add_y(GROUPS - 1, f)

            def norm_steps(j):
                dve.wait_ge(S["sum_done"], j + 1)
                for k in range(KT):
                    V.tensor_tensor(res[:, k, :], res[:, k, :], ps[:, (4, 0)[j], :], ALU.subtract)\
                        .then_inc(S["cz_ready"], 1)
                dve.wait_ge(S["sd_ready"], j + 1)
                V.reciprocal(rstd[:], rstd[:]).then_inc(S["lnr_ready"], 1)
                dve.wait_ge(S["lnr_ready"], j + 1)

            dve.wait_ge(S["y_added"], 16 * GROUPS)
            norm_steps(0)

            def u2_low(k):
                dve.wait_ge(S["u2h_ready"], k + 1)
                V.scalar_tensor_tensor(out=uL[:, k, :], in0=ring_n[k % 4][:], scalar=lnA[:, 1, k:k + 1],
                                       in1=uH[:, k, :].bitcast(F32), op0=ALU.add, op1=ALU.subtract)\
                    .then_inc(S["u2l_ready"], 1)

            for k in range(KT):
                if k >= 4:
                    dve.wait_ge(S["u2l_ready"], k - 3)
                V.scalar_tensor_tensor(out=ring_n[k % 4][:], in0=res[:, k, :], scalar=lnA[:, 0, k:k + 1],
                                       in1=rstd[:], op0=ALU.mult, op1=ALU.mult).then_inc(S["n_ready"], 1)
                if k >= 1:
                    u2_low(k - 1)
            u2_low(KT - 1)
            for k in range(KT):
                V.scalar_tensor_tensor(out=res[:, k, :], in0=res[:, k, :], scalar=lnA[:, 2, k:k + 1],
                                       in1=rstd[:], op0=ALU.mult, op1=ALU.mult).then_inc(S["z2_step"], 1)
                if k >= 1:
                    dve.wait_ge(S["z2_step"], k)
                    V.tensor_scalar(res[:, k - 1, :], res[:, k - 1, :], lnA[:, 3, k - 1:k], None, ALU.add)\
                        .then_inc(S["z2_added"], 1)
            dve.wait_ge(S["z2_step"], KT)
            V.tensor_scalar(res[:, KT - 1, :], res[:, KT - 1, :], lnA[:, 3, KT - 1:KT], None, ALU.add)\
                .then_inc(S["z2_added"], 1)

            def pair_steps(g, p):
                q = 4 * g + p
                for i in range(2):
                    dve.wait_ge(S["base_ready"], 2 * q + i + 1)
                    dst = yv if i == 0 else yg
                    for tap, lag in ((1, 1), (0, 2)):
                        col = V_CONV + 4 * i + 8 * p + tap
                        w = vecs[:, bass.ds(g * 32 + col, 1)]
                        if lag == 2:
                            dve.wait_ge(S["conv_step"], 4 * q + 2 * i + 1)
                        V.scalar_tensor_tensor(out=dst[:, p % 2, lag:T], in0=ps[:, 2 * (p % 2) + i, 0:T - lag],
                                               scalar=w, in1=dst[:, p % 2, lag:T], op0=ALU.mult,
                                               op1=ALU.add).then_inc(S["conv_step"], 1)
                dve.wait_ge(S["sil_ready"], q + 1)
                if p >= 2 or not isinstance(g, int):
                    dve.wait_ge(S["vl_ready"], q - 1)
                V.tensor_tensor(prod[:, p % 2, :], yv[:, p % 2, :], sgate[:, p % 2, :], ALU.mult)\
                    .then_inc(S["pr_ready"], 1)

            def pair_low(g, p):
                q = 4 * g + p
                dve.wait_ge(S["vh_ready"], q + 1)
                V.tensor_tensor(vL[:, p, :], prod[:, p % 2, :], vH[:, p, :].bitcast(F32), ALU.subtract)\
                    .then_inc(S["vl_ready"], 1)

            def down_steps(g):
                for f in range(KT):
                    dve.wait_ge(S["down_done"], 16 * g + f + 1)
                    dve.wait_ge(S["z2_added"], 16 * g + KT)
                    V.scalar_tensor_tensor(out=res[:, f, :], in0=ps[:, 4 + f % 4, :],
                                           scalar=mod1[:, 2, f:f + 1], in1=res[:, f, :], op0=ALU.mult,
                                           op1=ALU.add).then_inc(S["z2_added"], 1)

            for p in range(PAIRS):
                pair_steps(0, p)
                pair_low(0, p)
            with dve.Fori(1, FG) as g:
                pair_steps(g, 0)
                down_steps(g - 1)
                pair_low(g, 0)
                for p in range(1, PAIRS):
                    pair_steps(g, p)
                    pair_low(g, p)
            down_steps(FG - 1)
            dve.wait_ge(S["z2_added"], 16 * FG + KT)
            norm_steps(1)
            for k in range(KT):
                V.scalar_tensor_tensor(out=res[:, k, :], in0=res[:, k, :], scalar=vecs[:, V_LN2G + k:V_LN2G + k + 1],
                                       in1=rstd[:], op0=ALU.mult, op1=ALU.mult).then_inc(S["n_ready"], 1)

        @block.tensor
        def _(pe):
            def w3(s, n, cols):
                return (wH[s][:].rearrange("p (k n) -> p k n", n=cols),
                        wL[s][:].rearrange("p (k n) -> p k n", n=cols))

            def quarter(bank, s, kq):
                h, l = w3(s, KT, P)
                for k in range(4 * kq, 4 * kq + 4):
                    last = three(bank, h[:, k, :], l[:, k, :], uH[:, k, :], uL[:, k, :],
                                 k == 0, k == KT - 1)
                return last

            def values(k, h, l):
                for t in range(TT):
                    tok = slice(t * P, (t + 1) * P)
                    bank = ps[:, 2 + t // 2, (t % 2) * GW:(t % 2 + 1) * GW]
                    nc.tensor.matmul(bank, uH[:, k, tok], h, start=(k == 0 and t % 2 == 0),
                                     stop=False, skip_group_check=True)
                    nc.tensor.matmul(bank, uL[:, k, tok], h, start=False, stop=False,
                                     skip_group_check=True)
                    last = nc.tensor.matmul(bank, uH[:, k, tok], l, start=False,
                                            stop=(k == KT - 1), skip_group_check=True)
                return last

            for k in range(KT):
                n = k // 2
                if k % 2 == 0:
                    pe.wait_ge(S["w_lo"], n + 1)
                pe.wait_ge(S["ul_ready"], k + 1)
                h, l = (x[n % 2][:, 0:2 * FIRST_W].rearrange("p (k n) -> p k n", k=2)[:, k % 2, :]
                        for x in (wH, wL))
                for bank, at, m in ((0, 0, P), (1, P, P), (7, 6 * P, RANK), (2, 4 * P, GW),
                                    (4, 2 * P, P), (5, 3 * P, P)):
                    if bank == 2:
                        last = values(k, h[:, at:at + GW], l[:, at:at + GW])
                    else:
                        last = three(ps[0:m, bank, :], h[:, at:at + m], l[:, at:at + m], uH[:, k, :],
                                     uL[:, k, :], k == 0, k == KT - 1)
                    if k == KT - 1:
                        last.then_inc(S["first_done"], 1)
                if k % 2 == 1 and k < KT - 1:
                    last.then_inc(S["first_used"], 1)

            def projection_unit(w, u, i, b):
                kq = u % 4
                s = i % 2
                if kq == 0:
                    first = isinstance(w, int)
                    pe.wait_ge(S["w_lo"], PRO + i + 1 if first else 8 * w + (7 + i))
                    if b == 0:
                        pe.wait_ge(S["proj_evac"], 1 if first else 5 * w + 3)
                    elif b == 1 and first:
                        pe.wait_ge(S["proj_evac"], 2)
                    elif b == 2 and first:
                        pe.wait_ge(S["proj_evac"], 6)
                    elif b < 3:
                        pe.wait_ge(S["y_added"], 16 * w + (b - 2))
                    elif b == 3:
                        pe.wait_ge(S["proj_evac"], 5 * w + 7)
                    elif b == 4:
                        pe.wait_ge(S["proj_evac"], 5 * w + 5)
                if b < 4:
                    last = quarter(ps[:, b % 2, :], s, kq)
                else:
                    h, l = w3(s, 8, GW)
                    for kk in range(2 * kq, 2 * kq + 2):
                        last = values(8 * (b - 4) + kk, h[:, kk, :], l[:, kk, :])
                if kq == 3:
                    last.then_inc(S["proj_done"], 1)

            def wout(f, s, block, free, count):
                if f % 8 == 0:
                    pe.wait_ge(S["w_lo"], block)
                pe.wait_ge(free, count)
                h, l = (x[s][:].rearrange("p (k f n) -> p k f n", k=2, f=8) for x in (wH, wL))
                for k in range(2):
                    last = three(ps[:, (f + 1) % 2, :], h[:, k, f % 8, :], l[:, k, f % 8, :], oH[:, k, :],
                                 oL[:, k, :], k == 0, k == 1)
                last.then_inc(S["wout_done"], 1)

            def unit(w, u, layout):
                i = u // 4
                kind, b = layout[i]
                if kind == "p":
                    projection_unit(w, u, i, b)
                else:
                    if u == 4:
                        pe.wait_ge(S["ol_ready"], w)
                    for f in (2 * (u - 4), 2 * (u - 4) + 1):
                        if f < 2:
                            free, count = S["proj_evac"], 5 * w + (4 + 2 * f)
                        else:
                            free, count = S["y_added"], 16 * w + (f - 17)
                        wout(f, i % 2, 8 * w + (7 + i), free, count)

            def decays(w, c, j):
                cc = 4 * w + c
                if c == 0 and j < 2:
                    pe.wait_ge(S["la_ready"], w + 1)
                elif j < 2:
                    pe.wait_ge(S["exp_ready"], 3 * cc)
                else:
                    pe.wait_ge(S["exp_ready"], 3 * cc + 1)
                nc.tensor.matmul(ps[:, 4 + j % 2, 0:3 * P], la[:, c, :],
                                 dsum[:, 3 * j:3 * j + 3, :].rearrange("p s t -> p (s t)"),
                                 start=True, stop=True).then_inc(S["dsum_done"], 1)

            def scores(w, c, j):
                cc = 4 * w + c
                pe.wait_ge(S["qk_scaled"], 6 * cc + 2 * j + 2)
                if j == 0 and c > 0:
                    pe.wait_ge(S["masked"], 3 * cc)
                if j == 1 and c > 0:
                    pe.wait_ge(S["o_evac"], cc)
                if j == 2:
                    pe.wait_ge(S["masked"], 3 * cc + 1)
                tok = slice(c * P, (c + 1) * P)
                pairs = [(KE[:, 3 * j + i, :], Q[:, 3 * j + i, :]) for i in range(3 if j < 2 else 1)]
                if j == 2:
                    pairs.append((kw[:, tok], qw[:, tok]))
                for i, (k, q) in enumerate(pairs):
                    last = nc.tensor.matmul(ps[:, 6 + j % 2, i * P:(i + 1) * P], k, q, start=True, stop=True,
                                            skip_group_check=True)
                last.then_inc(S["score_done"], 1)

            def gla_output(w, c):
                cc = 4 * w + c
                pe.wait_ge(S["ssum_ready"], cc + 1)
                if c > 0:
                    pe.wait_ge(S["state_ready"], 3 * w + c)
                else:
                    pe.wait_ge(S["proj_evac"], 5 * w + 5)
                for d in range(2):
                    dv = slice(d * P, (d + 1) * P)
                    last = nc.tensor.matmul(ps[:, 7, dv], Vw[:, c, dv], ssum[:], start=True,
                                            stop=(c == 0), skip_group_check=True)
                    if c > 0:
                        last = nc.tensor.matmul(ps[:, 7, dv], state[:, dv], Q[:, 8, :], start=False,
                                                stop=True, skip_group_check=True)
                last.then_inc(S["gla_o_done"], 1)
                if c < 3:
                    pe.wait_ge(S["kht_ready"], 3 * w + c + 1)
                    nc.tensor.matmul(ps[:, 2, 0:GW], khT[:], Vw[:, c, :], start=True, stop=True)\
                        .then_inc(S["upd_done"], 1)

            def gla_window(w, layout):
                for u in range(4 * len(layout)):
                    if u == 1:
                        pe.wait_ge(S["wgate_in"], 16 * w + 16)
                        pe.wait_ge(S["glr_ready"], 1)
                        if isinstance(w, int):
                            pe.wait_ge(S["proj_evac"], 5)
                        for t in range(TT):
                            last = nc.tensor.matmul(ps[:, 4, t * P:(t + 1) * P], glr[:, t * P:(t + 1) * P],
                                                    wgate[:], start=True, stop=True, skip_group_check=True)
                        last.then_inc(S["logit_done"], 1)
                    c, step = (u - GLA_AT) // 4, (u - GLA_AT) % 4
                    if step == 0 and 1 <= c <= 4:
                        gla_output(w, c - 1)
                    if 0 <= c < 4:
                        if step == 0:
                            decays(w, c, 0)
                            decays(w, c, 1)
                        elif step == 1:
                            decays(w, c, 2)
                            scores(w, c, 0)
                        elif step == 2:
                            scores(w, c, 1)
                        else:
                            scores(w, c, 2)
                            if c < 3:
                                if c == 0:
                                    pe.wait_ge(S["proj_evac"], 5 * w + 5)
                                else:
                                    pe.wait_ge(S["kht_ready"], 3 * w + c)
                                nc.tensor.transpose(ps[:, 3, 0:P], KE[:, 8, :], ident[:])\
                                    .then_inc(S["kt_done"], 1)
                    if layout[u // 4] == ("p", 4) and u % 4 == 0:
                        pe.wait_ge(S["state_ready"], 3 * w + 3)
                        pe.wait_ge(S["kht_ready"], 3 * w + 3)
                    if u == MS_AT - 1:
                        pe.wait_ge(S["sq_ready"], w + 1)
                        for d in range(2):
                            last = nc.tensor.matmul(ps[:, 6, :], ones_rms[:], osq[:, d, :], start=(d == 0),
                                                    stop=(d == 1))
                        last.then_inc(S["ms_done"], 1)
                    unit(w, u, layout)

            pe.wait_ge(S["gla_const_in"], 64)
            gla_window(0, FIRST_LAYOUT)
            with pe.Fori(1, GLA) as w:
                gla_window(w, LAYOUT)

            def att_window(w, is_last):
                v = w - GLA
                pe.wait_ge(S["proj_evac"], 5 * w + 5)
                for u in range(32):
                    if u in S_AT:
                        k = S_AT[u]
                        h, i = k // 4, k % 4
                        pe.wait_ge(S["rot_step"], 16 * v + 8 * h + 8)
                        if k >= 2:
                            pe.wait_ge(S["o_evac"], 16 + 8 * v + k - 1)
                        nt = (i + 1) * P
                        nc.tensor.matmul(ps[:, 4 + k % 2, 0:nt], rot[:, 2 * h, i * P:nt],
                                         rot[:, 2 * h + 1, 0:nt], start=True, stop=True)\
                            .then_inc(S["s_done"], 1)
                    if u in T_AT:
                        k = T_AT[u]
                        pe.wait_ge(S["p_step"], 16 * v + 2 * k + 2)
                        if k >= 2:
                            pe.wait_ge(S["pt_ready"], 8 * v + k - 1)
                        for j in range(k % 4 + 1):
                            last = nc.tensor.transpose(ps[:, 6 + k % 2, j * P:(j + 1) * P],
                                                       Pm[:, k % 2, j * P:(j + 1) * P], ident[:])
                        last.then_inc(S["tr_done"], 1)
                    if u in A_AT:
                        k = A_AT[u]
                        h, i = k // 4, k % 4
                        pe.wait_ge(S["pt_ready"], 8 * v + k + 1)
                        for j in range(i + 1):
                            last = nc.tensor.matmul(ps[:, 4 + k % 2, 0:P], Vw[:, j, h * P:(h + 1) * P],
                                                    PT[:, k % 2, j * P:(j + 1) * P], start=(j == 0),
                                                    stop=(j == i), skip_group_check=True)
                        last.then_inc(S["ao_done"], 1)
                    if not is_last:
                        unit(w, u, LAYOUT)
                    elif FILL_AT <= u < FILL_AT + KT:
                        f = u - FILL_AT
                        if f == 0:
                            pe.wait_ge(S["ol_ready"], w)
                        wout(f, f // 8, FFN0 - 4 + f // 8 + 1,
                             *((S["proj_evac"], 5 * w + (4 - f)) if f < 2
                               else (S["y_added"], 16 * w + (f - 17))))

            with pe.Fori(GLA, GROUPS - 1) as w:
                att_window(w, False)
            last_w = GROUPS - 1
            att_window(last_w, True)
            pe.wait_ge(S["ol_ready"], GROUPS)
            for f in range(KT):
                wout(f, f // 8, FFN0 - 2 + f // 8 + 1, S["y_added"], 16 * last_w + (f - 1))

            def norm_steps(j):
                pe.wait_ge(S["zsum_step"], (KT - 1) * (j + 1))
                nc.tensor.matmul(ps[:, (4, 0)[j], :], ones_ln[:], zsum[:], start=True, stop=True)\
                    .then_inc(S["sum_done"], 1)
                for k in range(KT):
                    pe.wait_ge(S["csq_ready"], KT * j + k + 1)
                    nc.tensor.matmul(ps[:, (5, 1)[j], :], ones_ln[:], ring_n[k % 4][:], start=(k == 0),
                                     stop=(k == KT - 1)).then_inc(S["var_done"], 1)

            norm_steps(0)

            def up(g, p, i, n_wait, s):
                q = 4 * g + p
                pe.wait_ge(S["w_lo"], n_wait)
                if p >= 2 or not isinstance(g, int):
                    pe.wait_ge(S["conv_step"], 4 * q + (2 * i - 6))
                h, l = w3(s, KT, P)
                bank = ps[:, 2 * (p % 2) + i, :]
                for k in range(KT):
                    last = three(bank, h[:, k, :], l[:, k, :], uH[:, k, :], uL[:, k, :], k == 0, k == KT - 1)
                last.then_inc(S["up_done"], 1)

            def down(g, n_off):
                pe.wait_ge(S["vl_ready"], 4 * g + PAIRS)
                for f in range(KT):
                    d = f // 4
                    s = (n_off + d) % 2
                    if f % 4 == 0:
                        pe.wait_ge(S["w_lo"], 12 * g + (n_off + d + 1))
                        h, l = (x[s][:].rearrange("p (k f n) -> p k f n", k=4, f=4) for x in (wH, wL))
                    pe.wait_ge(S["z2_added"], 16 * g + (KT if f < 4 else KT + f - 3))
                    for k in range(4):
                        last = three(ps[:, 4 + f % 4, :], h[:, k, f % 4, :], l[:, k, f % 4, :], vH[:, k, :],
                                     vL[:, k, :], k == 0, k == 3)
                    last.then_inc(S["down_done"], 1)

            pe.wait_ge(S["w_lo"], FFN0 + 2)
            for k in range(KT):
                pe.wait_ge(S["u2l_ready"], k + 1)
                for i in range(2):
                    h, l = w3(i, KT, P)
                    last = three(ps[:, i, :], h[:, k, :], l[:, k, :], uH[:, k, :], uL[:, k, :],
                                 k == 0, k == KT - 1)
                    if k == KT - 1:
                        last.then_inc(S["up_done"], 1)
            for p in range(1, PAIRS):
                for i in range(2):
                    n = FFN0 + 2 * p + i
                    up(0, p, i, n + 1, n % 2)
            with pe.Fori(1, FG) as g:
                for i in range(12):
                    m = FFN0 - 4 + i
                    if 2 <= i < 6:
                        if i == 2:
                            down(g - 1, FFN0 - 4 + 2 + 12)
                        continue
                    p = 0 if i < 2 else (i - 4) // 2
                    up(g, p, i % 2, 12 * g + (m + 1), m % 2)
            down(FG - 1, FFN0 - 4 + 12)
            norm_steps(1)


def level_constants():
    t = np.arange(P)
    sums = np.zeros((P, SETS, P), np.float32)
    masks = np.zeros((P, LEVELS + 1, P), np.float32)
    tp = t[:, None]
    tq = t[None, :]
    for level in range(LEVELS):
        half = P >> (level + 1)
        mid = tq // (2 * half) * (2 * half) + half - 1
        late = tq % (2 * half) >= half
        span = np.where(late, (tp > mid) & (tp <= tq), (tp > tq) & (tp <= mid))
        sums[:, level, :] = span / TAU
        same = tp // (2 * half) == tq // (2 * half)
        masks[:, level, :] = same & late & (tp % (2 * half) < half)
    sums[:, LEVELS, :] = (tp <= tq) / TAU
    sums[:, LEVELS + 1, :] = (tp > tq) / TAU
    masks[:, LEVELS, :] = tp == tq
    return sums, masks


def band_constants():
    dist = (3 * P + np.arange(P))[:, None] - np.arange(T)[None, :]
    count = ((dist >= 0) & (dist <= 128)).astype(int)
    count += (dist >= 0) & (dist <= 512) & (dist % 4 == 0)
    count += (dist >= 0) & (dist <= 2048) & (dist % 16 == 0)
    return np.where(count > 0, np.log(np.maximum(count, 1)), -1e30).astype(np.float32)


def kernel(x, c, positions, w_ada, b_ada, w_in, w_gla_gate, b_gla_gate, gla_norm_g, w_out, ln1_g, ln1_b,
           w_up, conv_w, conv_b, w_down, ln2_g, ln2_b):
    import concourse.bacc as bacc
    from concourse.bass_utils import run_bass_kernel_spmd

    f32 = np.float32
    x, w_ada, w_in, w_out, w_up, w_down = (np.asarray(a) for a in (x, w_ada, w_in, w_out, w_up, w_down))
    x_t = np.ascontiguousarray(x[0].T.reshape(KT, P, T).transpose(1, 0, 2))

    def tiles(w):
        return w.reshape(-1, P, w.shape[1]).transpose(1, 0, 2)

    wi, wo, wu, wd = w_in[0], w_out[0], w_up[0], w_down[0]
    gk, ga = 4 * P, 8 * P
    off_k, off_v, off_g, off_lr = gk, 2 * gk, 2 * gk + ga, 2 * gk + 2 * ga
    off_aq = off_lr + RANK
    off_ak, off_av = off_aq + ga, off_aq + 2 * ga

    def projection(group):
        if group < GLA:
            at = [group * P, off_k + group * P, off_g + group * GW, off_g + group * GW + P]
            v = off_v + group * GW
        else:
            h = 2 * (group - GLA)
            at = [off_aq + h * P, off_ak + h * P, off_aq + (h + 1) * P, off_ak + (h + 1) * P]
            v = off_av + h * P
        blocks = [tiles(wi[:, a:a + P]) for a in at]
        values = tiles(wi[:, v:v + GW])
        return blocks + [values[:, 0:8], values[:, 8:16]]

    def output(group):
        rows = tiles(wo[group * GW:(group + 1) * GW])
        return [rows[:, :, d * 1024:(d + 1) * 1024] for d in range(2)]

    def up(f):
        return [tiles(wu[:, f * P:(f + 1) * P]), tiles(wu[:, DFF + f * P:DFF + (f + 1) * P])]

    def down(g):
        rows = tiles(wd[g * PAIRS * P:(g + 1) * PAIRS * P])
        return [rows[:, :, d * 512:(d + 1) * 512] for d in range(4)]

    columns_0 = [slice(a, a + n) for a, n in ((0, P), (off_k, P), (off_g, GW), (off_v, GW), (off_lr, RANK))]
    first = tiles(np.concatenate([wi[:, c] for c in columns_0], axis=1))
    w_first = np.ascontiguousarray(first.reshape(P, PRO, 2 * FIRST_W).transpose(1, 0, 2))
    blocks = projection(1)
    for w in range(1, GROUPS):
        if w + 1 < GROUPS:
            proj = projection(w + 1)
            blocks += proj[:1] + output(w - 1) + proj[1:]
        else:
            blocks += output(w - 1) + output(w)
    for p in range(PAIRS):
        blocks += up(p)
    for g in range(1, FG):
        blocks += up(PAIRS * g) + down(g - 1)
        for p in range(1, PAIRS):
            blocks += up(PAIRS * g + p)
    blocks += down(FG - 1)
    assert len(blocks) == NBLK - PRO
    w_stream = np.empty((NBLK - PRO, P, WBLK), f32)
    for n, b in enumerate(blocks):
        w_stream[n] = b.reshape(P, WBLK)

    w_ada_t = np.ascontiguousarray(w_ada[0].T).reshape(6 * D // P, P, D)
    w_gate = np.concatenate([np.asarray(w_gla_gate)[0], np.asarray(b_gla_gate)[0][None]])
    w_gate = np.ascontiguousarray(w_gate.reshape(RANK + 1, GLA, P).transpose(1, 0, 2))

    def columns(v):
        return np.asarray(v).reshape(-1, P).T

    vec = np.zeros((P, NVEC), f32)
    vec[:, V_BADA:V_BADA + 96] = columns(b_ada[0])
    for at, v in ((V_LN1G, ln1_g), (V_LN1B, ln1_b), (V_LN2G, ln2_g), (V_LN2B, ln2_b)):
        vec[:, at:at + KT] = columns(v[0])
    vec[:, V_GNORM:V_GNORM + 2] = columns(gla_norm_g[0])
    half = np.arange(64, dtype=f32)
    inv_freq = (f32(10000.0) ** (-half / f32(64))).astype(f32)
    vec[:, V_INVF] = np.concatenate([inv_freq, inv_freq])
    vec[:, V_SGN] = np.repeat([1.0, -1.0], 64)
    vec[:, V_EPS] = RMS_EPS
    vec[:, V_EPS + 1] = LN_EPS
    vec[:, V_EPS + 2] = 1.0
    conv = np.concatenate([np.asarray(conv_w)[0], np.asarray(conv_b)[0][None]])
    conv = conv.reshape(4, 2, FT, P).transpose(3, 2, 1, 0)
    vec[:, V_CONV:V_CONV + FT * 8] = conv.reshape(P, FT * 8)

    sums, masks = level_constants()
    eye = np.zeros((P, 3, P), f32)
    eye[:, 0, :] = np.eye(P)
    eye[:, 1, :] = 1.0 / GW
    eye[:, 2, :] = 1.0 / D
    arrays = {
        "x": x_t,
        "c_rows": np.ascontiguousarray(np.broadcast_to(np.asarray(c)[0], (P, D))),
        "pos_rows": np.ascontiguousarray(np.broadcast_to(np.asarray(positions)[0], (P, T))),
        "w_first": w_first, "w_stream": w_stream, "w_ada_t": w_ada_t, "w_gate": w_gate, "vec": vec,
        "decay_sums": sums, "level_masks": masks, "band_bias": band_constants(), "eye": eye,
    }
    nc = bacc.Bacc("TRN2", target_bir_lowering=False, num_devices=1, dynamic_dma_scratch_size=1024)
    args = [nc.dram_tensor(n, a.shape, mybir.dt.from_np(a.dtype), kind="ExternalInput").ap()
            for n, a in arrays.items()]
    out = nc.dram_tensor("out", (P, KT, T), F32, kind="ExternalOutput").ap()
    build(nc, *args, out)
    got = run_bass_kernel_spmd(nc, [arrays], core_ids=[0]).results[0]["out"]
    return np.ascontiguousarray(got.transpose(1, 0, 2).reshape(D, T).T)[None]
```

```python
import math

import numpy as np

import concourse.bass as bass
from concourse import mybir
from concourse.alu_op_type import AluOpType as ALU

ACT = mybir.ActivationFunctionType
F32 = mybir.dt.float32
F32R = mybir.dt.float32r
I32 = mybir.dt.int32
AX_X = mybir.AxisListType.X

P = 128
D = 2048
T = 512
KT = D // P
TT = T // P
DFF = 5632
FT = DFF // P
GROUPS = 8
GLA = 4
GW = D // GROUPS
RANK = 16
TAU = 16.0
SCALE = 128.0 ** -0.5
ALPHA = 2.0 ** 0.25
LN_EPS, RMS_EPS = 1e-5, 1e-6
WBLK = 2048
LEVELS = 7
SETS = LEVELS + 2
FIRST_W = 6 * P + RANK
PRO = KT // 2
FFN0 = PRO + 8 * GROUPS - 6
PAIRS = 4
FG = FT // PAIRS
NBLK = FFN0 + FG * 12
ADA_SLOTS = 4
SHIFT1, SCALE1, GATE1, SHIFT2, SCALE2, GATE2 = range(0, 96, 16)

V_BADA, V_LN1G, V_LN1B, V_LN2G, V_LN2B = 0, 96, 112, 128, 144
V_GNORM, V_INVF, V_SGN, V_EPS, V_CONV = 160, 162, 163, 164, 168
NVEC = V_CONV + FT * 8

FIRST_LAYOUT = [("p", b) for b in range(6)]
LAYOUT = [("p", 0), ("o", 0), ("o", 1)] + [("p", b) for b in range(1, 6)]
LOGITS_AT = {len(FIRST_LAYOUT): 1, len(LAYOUT): 0}
GLA_AT, SQ_AT, MS_AT, O_AT = 3, 19, 22, 23
S_AT = {3 * k + 4: k for k in range(8)}
T_AT = {3 * k + 7: k for k in range(8)}
A_AT = {3 * k + 9: k for k in range(8)}
ROT_AT = {17: 0, 20: 1, 26: 2, 29: 3}
PAIR_AT = 31
FILL_AT = {5 + f * 5 // 3: f for f in range(KT)}
ADA_FIRST_AT = [h * 2 // 3 for h in range(32)]
HALF_SLOTS = 3
SLOT0_LOADS = len(range(0, len(ADA_FIRST_AT), HALF_SLOTS))
ADA_AT = list(range(0, 32, 2))


SQ_PAIRS = 7
VAR_STEPS = KT - SQ_PAIRS
POOL_TILES = list(range(2, KT, 3))
DVE_TILES = [k for k in range(KT) if k not in POOL_TILES]


def build(nc, x, c_in, pos_rows, w_first, w_stream, w_ada_t, w_gate, vec, decay_sums, level_masks,
          band_bias, eye, out):
    used = [nc.sbuf_base + 31 - (nc.sbuf_base + 31) % 32]

    def sb(name, shape, dt, at=None):
        size = int(np.prod(shape[1:])) * 4
        if at is None:
            at = used[0]
            used[0] += (size + 31) // 32 * 32
            assert used[0] <= nc.sbuf_usable_end, (name, used[0])
        tile = nc.alloc_sbuf_tensor_at(name, shape, dt, offset=at)
        where[name] = at
        return tile

    where = {}
    res = sb("res", [P, KT, T], F32)
    uH = sb("uH", [P, KT, T], F32R)
    uL = sb("uL", [P, KT, T], F32R)
    raw = [sb(f"raw{s}", [P, WBLK], F32) for s in range(2)]
    wH = [sb(f"wH{s}", [P, WBLK], F32R) for s in range(2)]
    wL = [sb(f"wL{s}", [P, WBLK], F32R) for s in range(2)]
    c_row = sb("c_row", [P, D], F32, at=where["wL1"])
    ones_row = sb("ones_row", [P, P], F32, at=where["wL0"])
    ada_half = [sb("ada_half0", [P, WBLK // 2], F32)]
    csil = sb("csil", [P, D], F32)
    vecs = sb("vecs", [P, NVEC], F32)
    mod = sb("mod", [P, 96], F32)
    mod1 = sb("mod1", [P, 3, KT], F32)
    acc = sb("acc", [P, 32], F32)
    root1 = sb("root1", [P, 2], F32)
    acc16 = sb("acc16", [P, 16], F32)
    lnA = sb("lnA", [P, 4, KT], F32)
    ident = sb("ident", [P, P], F32)
    ones_rms = sb("ones_rms", [P, P], F32)
    ones_ln = sb("ones_ln", [P, P], F32)
    mixer0 = used[0]
    stage = sb("stage", [P, 4, T], F32)
    Vw = sb("Vw", [P, TT, GW], F32)
    oH = sb("oH", [P, 2, T], F32R)
    oL = sb("oL", [P, 2, T], F32R)
    dsum = sb("dsum", [P, SETS, P], F32)
    dsumR = sb("dsumR", [P, SETS, P], F32R, at=where["dsum"])
    masks = sb("masks", [P, LEVELS + 1, P], F32)
    cosT = sb("cosT", [P, T], F32)
    sinT = sb("sinT", [P, T], F32)
    bias = sb("bias", [P, T], F32)
    work0 = used[0]
    glr = sb("glr", [RANK + 1, T], F32)
    wgate = sb("wgate", [RANK + 1, P], F32)
    laH = sb("laH", [P, TT, P], F32R)
    qw = sb("qw", [P, T], F32)
    kw = sb("kw", [P, T], F32)
    sg = sb("sg", [P, 2, T], F32)
    KE = sb("KE", [P, SETS, P], F32)
    Q = sb("Q", [P, SETS, P], F32)
    ssum = sb("ssum", [P, P], F32)
    state = sb("state", [P, GW], F32)
    khT = sb("khT", [P, P], F32)
    o = sb("o", [P, 2, T], F32)
    la = sb("la", [P, TT, P], F32, at=where["KE"])
    laL = sb("laL", [P, TT, P], F32R, at=where["bias"])
    absz = sb("absz", [P, T], F32, at=where["Q"])
    softp = sb("softp", [P, T], F32, at=where["Q"] + T * 4)
    osq = sb("osq", [P, 2, T], F32, at=where["Q"])
    rms = sb("rms", [P, T], F32, at=where["KE"])
    def over(name, shape, dt, off):
        assert work0 + off + int(np.prod(shape[1:])) * 4 <= used[0], name
        return sb(name, shape, dt, at=work0 + off)
    rot = over("rot", [P, 4, T], F32, 2048)
    rtmp = over("rtmp", [P, 2, T], F32, 10240)
    Pm = over("Pm", [P, 2, T], F32, 14336)
    PT = over("PT", [P, 2, T], F32, 18432)
    astat = over("astat", [P, 2, 4], F32, 22528)
    ring_u = [over(f"ring_u{s}", [P, T], F32, 2560 + s * 2048) for s in range(4)]
    ada_big = [sb("ada_big0", [P, WBLK], F32, at=where["stage"]),
               sb("ada_big1", [P, WBLK], F32, at=where["Vw"])]
    ada_big += [over(f"ada_big{s}", [P, WBLK], F32, 10752 + (s - 2) * WBLK * 4) for s in (2, 3)]
    assert where["oL"] >= where["Vw"] + WBLK * 4
    posi = sb("posi", [P, T], I32, at=where["cosT"])
    ang = sb("ang", [P, T], F32, at=where["oL"])
    turns = sb("turns", [P, T], F32, at=where["oL"] + T * 4)
    ada_half += [sb("ada_half1", [P, WBLK // 2], F32, at=where["oL"]),
                 sb("ada_half2", [P, WBLK // 2], F32, at=where["oH"])]
    sofar = used[0]
    used[0] = mixer0
    vH = sb("vH", [P, PAIRS, T], F32R)
    vL = sb("vL", [P, PAIRS, T], F32R)
    yv = sb("yv", [P, 2, T], F32)
    yg = sb("yg", [P, 2, T], F32)
    sgate = sb("sgate", [P, 2, T], F32)
    prod = sb("prod", [P, 2, T], F32)
    ring_n = [sb(f"ring_n{s}", [P, T], F32) for s in range(8)]
    rstd = sb("rstd", [P, T], F32)
    zsum = sb("zsum", [P, 2, T], F32)
    used[0] = max(used[0], sofar)

    ps = nc.alloc_psum_tensor("ps", [P, 8, T], F32)

    names = """c_in ones_ready c_spread const_in pos_in gla_const_in att_const_in wgate_in out_done
        w_hi w_lo silu_c ada_dot ada_half_dot mod_step
        uf_ready uh_ready ul_ready ax_ready first_used first_done
        proj_done proj_evac glr_ready glr_ones wout_done y_added
        logit_done abs_ready nexp_ready softp_ready la_ready lah_ready lal_ready dsum_ready gla_qk
        dsum_done exp_ready qk_scaled score_done masked ssum_ready
        kt_done kht_ready upd_done state_ready gla_o_done o_evac
        gate_ready sq_ready sq_added ms_done rt_ready rstd_ready o_step oh_ready ol_ready
        pos_step rot_step s_done biased neg_ready p_exp p_step tr_done pt_ready ao_done
        zsum_step zsum2_step sum_done cz_ready pair_ready pool_n_ready csq_ready
        var_done sd_ready lnr_ready ln_vec n_ready n2_ready u2h_ready u2l_ready
        up_done base_ready conv_step sil_ready pr_ready vh_ready vl_ready down_done z2_step z2_added
        fin_ready""".split()
    S = {n: nc.alloc_semaphore(n) for n in names}
    ada_big_in = [nc.alloc_semaphore(f"ada_big{s}_in") for s in range(ADA_SLOTS)]
    ada_half_in = [nc.alloc_semaphore(f"ada_half{s}_in") for s in range(HALF_SLOTS)]
    x_in = [nc.alloc_semaphore(f"x{q}_in") for q in range(4)]
    raw_in = [nc.alloc_semaphore(f"raw{s}_in") for s in range(2)]

    def three(bank, wh, wl, ah, al, first, last):
        nc.tensor.matmul(bank, wh, ah, start=first, stop=False, skip_group_check=True)
        nc.tensor.matmul(bank, wh, al, start=False, stop=False, skip_group_check=True)
        return nc.tensor.matmul(bank, wl, ah, start=False, stop=last, skip_group_check=True)

    with nc.Block() as block:
        @block.sync
        def _(sp):
            def load_raw(n, n_const, slot):
                sp.wait_ge(S["w_lo"], n + (n_const - 1))
                sp.dma_start(raw[slot][:], w_stream[n + (n_const - PRO)]).then_inc(raw_in[slot], 16)

            sp.dma_start(c_row[0:1, :], c_in).then_inc(S["c_in"], 16)
            sp.dma_start(vecs[:], vec).then_inc(S["const_in"], 16)
            for k in range(KT):
                for i, part in enumerate((SHIFT1, SCALE1)):
                    m = 2 * k + i
                    if m >= ADA_SLOTS:
                        sp.wait_ge(S["ada_dot"], m + 1 - ADA_SLOTS)
                    sp.dma_start(ada_big[m % ADA_SLOTS][:], w_ada_t[part + k])\
                        .then_inc(ada_big_in[m % ADA_SLOTS], 16)
                if k % 4 == 0:
                    sp.dma_start(res[:, k:k + 4, :], x[:, k:k + 4, :]).then_inc(x_in[k // 4], 16)
                if k % 2 == 0:
                    n = k // 2
                    if n >= 2:
                        sp.wait_ge(S["w_lo"], n - 1)
                    sp.dma_start(raw[n % 2][:, 0:2 * FIRST_W], w_first[n]).then_inc(raw_in[n % 2], 16)
                if k == 8:
                    sp.dma_start(posi[:], pos_rows).then_inc(S["pos_in"], 16)
            load_raw(PRO, 0, 0)
            sp.dma_start(wgate[:], w_gate[0]).then_inc(S["wgate_in"], 16)
            sp.dma_start(dsum[:], decay_sums).then_inc(S["gla_const_in"], 16)
            sp.dma_start(masks[:], level_masks).then_inc(S["gla_const_in"], 16)
            sp.dma_start(ident[:], eye[:, 0, :]).then_inc(S["gla_const_in"], 16)
            sp.dma_start(ones_rms[:], eye[:, 1, :]).then_inc(S["gla_const_in"], 16)
            load_raw(PRO, 1, 1)
            load_raw(PRO, 2, 0)
            sp.wait_ge(S["pos_step"], 13)

            def gate_weights(w):
                sp.wait_ge(S["logit_done"], w + 1)
                sp.dma_start(wgate[:], w_gate[w + 1]).then_inc(S["wgate_in"], 16)

            for i in range(-1, 6):
                for h, u in enumerate(ADA_FIRST_AT):
                    if u // 4 == i + 1:
                        s = h % HALF_SLOTS
                        if h >= HALF_SLOTS:
                            sp.wait_ge(S["ada_half_dot"], h + 1 - HALF_SLOTS)
                        sp.dma_start(ada_half[s][:], w_ada_t[GATE1 + h // 2][:, h % 2 * 1024:(h % 2 + 1) * 1024])\
                            .then_inc(ada_half_in[s], 16)
                load_raw(PRO, i + 4, (i + 4) % 2)
                if i == 1:
                    gate_weights(0)
            sp.dma_start(ones_ln[:], eye[:, 2, :]).then_inc(S["att_const_in"], 16)

            def window(w, more_gates=False):
                for i in range(8):
                    load_raw(8 * w, 10 + i, i % 2)
                    if i == 3 and more_gates:
                        gate_weights(w)

            with sp.Fori(1, GLA - 1) as w:
                window(w, True)
            with sp.Fori(GLA - 1, GROUPS - 1) as w:
                window(w)
            with sp.Fori(FFN0, NBLK - 1, 2) as n:
                load_raw(n, 0, 0)
                load_raw(n, 1, 1)
            for k in range(KT):
                sp.wait_ge(S["fin_ready"], k + 1)
                sp.dma_start(out[:, k, :], res[:, k, :]).then_inc(S["out_done"], 16)
            sp.wait_ge(S["out_done"], 16 * KT)

        @block.gpsimd
        def _(pool):
            def low(n, s, size=WBLK):
                pool.wait_ge(S["w_hi"], n + 1)
                nc.gpsimd.tensor_tensor(wL[s][:, 0:size], raw[s][:, 0:size], wH[s][:, 0:size].bitcast(F32),
                                        ALU.subtract).then_inc(S["w_lo"], 1)

            def add_tile(j, f, source, count):
                pool.wait_ge(source, count + f + 1)
                if f == 1:
                    first = res[:, 0, :]
                else:
                    pool.wait_ge(S["zsum_step"], 7 * j + f - 1)
                    first = zsum[:, 0, :]
                nc.gpsimd.tensor_tensor(zsum[:, 0, :], first, res[:, f, :], ALU.add)\
                    .then_inc(S["zsum_step"], 1)

            def add_squares(j):
                for i in range(SQ_PAIRS):
                    pool.wait_ge(S["csq_ready"], KT * j + 2 * i + 2)
                    nc.gpsimd.tensor_tensor(ring_n[2 * i % 8][:], ring_n[2 * i % 8][:],
                                            ring_n[(2 * i + 1) % 8][:], ALU.add)\
                        .then_inc(S["pair_ready"], 1)

            with pool.Fori(0, PRO - 1, 2) as n:
                low(n, 0, 2 * FIRST_W)
                low(n + 1, 1, 2 * FIRST_W)
            with pool.Fori(PRO, FFN0 - 1, 2) as n:
                low(n, 0)
                low(n + 1, 1)
            for f in range(1, 8):
                add_tile(0, f, S["y_added"], 16 * (GROUPS - 1))
            add_squares(0)
            with pool.Fori(FFN0, NBLK - 3, 2) as n:
                low(n, 0)
                low(n + 1, 1)
            for d in range(2):
                for f in range(max(1, 4 * d), 4 * d + 4):
                    add_tile(1, f, S["z2_added"], 16 * FG)
                low(NBLK - 2 + d, d)
            add_squares(1)
            pool.wait_ge(S["lnr_ready"], 2)
            for k in POOL_TILES:
                nc.gpsimd.tensor_tensor(res[:, k, :], res[:, k, :], rstd[:], ALU.mult)\
                    .then_inc(S["pool_n_ready"], 1)

        @block.scalar
        def _(act):
            def high(s, landed, freed=None, count=None, size=WBLK):
                act.wait_ge(raw_in[s], landed)
                if freed is not None:
                    act.wait_ge(freed, count)
                nc.scalar.activation(wH[s][:, 0:size], raw[s][:, 0:size], ACT.Copy).then_inc(S["w_hi"], 1)

            def landed(n):
                return 16 * (n // 2 + 1)

            def high_in_window(w, i, layout):
                kind, b = layout[i]
                at = landed(PRO + 2 + i) if layout is FIRST_LAYOUT else 64 * w + landed(8 + i)
                if kind == "p":
                    high(i % 2, at, S["proj_done"], 6 * w + (b + 1))
                else:
                    high(i % 2, at, S["wout_done"], 16 * w + (8 * b - 8))

            def load_ada(w, u):
                if u in ADA_AT:
                    h = ADA_AT.index(u)
                    act.wait_ge(S["ada_half_dot"], 16 * w + (16 + h))
                    act.dma_start(ada_half[0][:], w_ada_t[w * 8 + (SHIFT2 - 8 + h // 2)]
                                  [:, h % 2 * 1024:(h % 2 + 1) * 1024]).then_inc(ada_half_in[0], 16)

            def evac(w, b, bank=None):
                if b < 4:
                    bank = b % 2 if bank is None else bank
                    nc.scalar.activation(stage[:, b, :], ps[:, bank, :], ACT.Copy)\
                        .then_inc(S["proj_evac"], 1)
                else:
                    nc.scalar.activation(Vw[:].rearrange("p t v -> p (t v)"),
                                         ps[:, 2:4, :].rearrange("p b v -> p (b v)"), ACT.Copy)\
                        .then_inc(S["proj_evac"], 1)

            def evac_in_window(w, b, free):
                act.wait_ge(S["proj_done"], 6 * w + ((b if b < 4 else 5) + 1))
                if free is not None:
                    act.wait_ge(*free)
                evac(w, b)

            act.wait_ge(S["c_spread"], 1)
            nc.scalar.activation(csil[:], ps[:, 0:4, :].rearrange("p b t -> p (b t)"), ACT.Silu)\
                .then_inc(S["silu_c"], 1)
            act.wait_ge(S["const_in"], 16)
            high(0, landed(0), size=2 * FIRST_W)
            for k in range(KT):
                act.wait_ge(S["uf_ready"], k + 1)
                nc.scalar.activation(uH[:, k, :], ring_u[k % 4][:], ACT.Identity, bias=mod[:, k:k + 1])\
                    .then_inc(S["uh_ready"], 1)
                nc.scalar.activation(res[:, k, :], res[:, k, :], ACT.Copy, scale=ALPHA)\
                    .then_inc(S["ax_ready"], 1)
                if k == 0:
                    high(1, landed(1), size=2 * FIRST_W)
                elif k % 2 == 0 or k == KT - 1:
                    n = k // 2 + 1
                    if n < PRO or k == KT - 1:
                        high(n % 2, landed(n), S["first_used"], n - 1, 2 * FIRST_W if n < PRO else WBLK)
                if k == 11:
                    act.wait_ge(S["pos_step"], 10)
                    nc.scalar.activation(sinT[:], ang[:], ACT.Sin).then_inc(S["rt_ready"], 1)
                    nc.scalar.activation(cosT[:], ang[:], ACT.Sin, scale=0.5).then_inc(S["rt_ready"], 1)
            act.wait_ge(S["first_done"], 1)
            evac(-1, 0, 0)
            act.wait_ge(S["first_done"], 2)
            evac(-1, 1, 1)
            act.wait_ge(S["first_done"], 3)
            act.wait_ge(S["glr_ones"], 1)
            nc.scalar.activation(glr[0:RANK, :], ps[0:RANK, 7, :], ACT.Copy).then_inc(S["glr_ready"], 1)
            act.wait_ge(S["first_done"], 5)
            evac(-1, 2, 4)
            act.wait_ge(S["first_done"], 6)
            evac(-1, 3, 5)
            high(1, landed(PRO + 1), S["first_done"], 6)
            evac(-1, 4)

            def gla_window(w, layout):
                units = 4 * len(layout)
                for u in range(units):
                    if u == LOGITS_AT[len(layout)]:
                        act.wait_ge(S["logit_done"], w + 1)
                        nc.scalar.activation(absz[:], ps[:, 4, :], ACT.Abs).then_inc(S["abs_ready"], 1)
                        act.wait_ge(S["abs_ready"], w + 1)
                        nc.scalar.activation(softp[:], absz[:], ACT.Exp, scale=-1.0).then_inc(S["nexp_ready"], 1)
                        act.wait_ge(S["nexp_ready"], w + 1)
                        nc.scalar.activation(absz[:], softp[:], ACT.Ln, bias=vecs[:, V_EPS + 2:V_EPS + 3])\
                            .then_inc(S["softp_ready"], 1)
                    c, step = (u - GLA_AT) // 4, (u - GLA_AT) % 4
                    cc = 4 * w + c
                    if u == LOGITS_AT[len(layout)] + 1:
                        act.wait_ge(S["la_ready"], w + 1)
                        if not isinstance(w, int):
                            act.wait_ge(S["dsum_done"], 12 * w)
                        nc.scalar.activation(laH[:], la[:], ACT.Copy).then_inc(S["lah_ready"], 1)
                    if 0 <= c < 4:
                        if step == 0:
                            for j in range(2):
                                act.wait_ge(S["dsum_done"], 3 * cc + j + 1)
                                if c > 0:
                                    act.wait_ge(S["score_done"], 3 * cc + (j - 2))
                                elif j == 0:
                                    act.wait_ge(S["lal_ready"], w + 1)
                                nc.scalar.activation(KE[:, 3 * j:3 * j + 3, :].rearrange("p s t -> p (s t)"),
                                                     ps[:, 4 + j, 0:3 * P], ACT.Exp).then_inc(S["exp_ready"], 1)
                        if step == 1:
                            act.wait_ge(S["dsum_done"], 3 * cc + 3)
                            if c > 0:
                                act.wait_ge(S["score_done"], 3 * cc)
                                act.wait_ge(S["kt_done"], 3 * w + c)
                                if c > 1:
                                    act.wait_ge(S["state_ready"], 3 * w + c)
                            nc.scalar.activation(KE[:, 6:9, :].rearrange("p s t -> p (s t)"),
                                                 ps[:, 4, 0:3 * P], ACT.Exp).then_inc(S["exp_ready"], 1)
                        if step == 3 and c < 3:
                            act.wait_ge(S["kt_done"], 3 * w + c + 1)
                            if c > 0:
                                act.wait_ge(S["upd_done"], 3 * w + c)
                            nc.scalar.activation(khT[:], ps[:, 3, 0:P], ACT.Copy).then_inc(S["kht_ready"], 1)
                    if step == 0 and 1 <= c <= 4:
                        act.wait_ge(S["gla_o_done"], 4 * w + c)
                        nc.scalar.activation(o[:, :, (c - 1) * P:c * P],
                                             ps[:, 7, 0:GW].rearrange("p (d t) -> p d t", d=2),
                                             ACT.Copy).then_inc(S["o_evac"], 1)
                    if u == 10:
                        nc.scalar.activation(sg[:].rearrange("p d t -> p (d t)"),
                                             stage[:, 2:4, :].rearrange("p d t -> p (d t)"), ACT.Silu)\
                            .then_inc(S["gate_ready"], 1)
                    if u == SQ_AT:
                        act.wait_ge(S["o_evac"], 4 * w + 4)
                        act.wait_ge(S["ssum_ready"], 4 * w + 4)
                        nc.scalar.activation(osq[:], o[:], ACT.Square).then_inc(S["sq_ready"], 1)
                    if u == MS_AT:
                        act.wait_ge(S["ms_done"], w + 1)
                        nc.scalar.activation(rms[:], ps[:, 6, :], ACT.Sqrt, bias=vecs[:, V_EPS:V_EPS + 1])\
                            .then_inc(S["rt_ready"], 1)
                    if u == O_AT:
                        act.wait_ge(S["o_step"], 3 * w + 3)
                        nc.scalar.activation(oH[:], o[:], ACT.Copy).then_inc(S["oh_ready"], 1)
                    if layout is LAYOUT:
                        load_ada(w, u)
                    if u % 4 == 3:
                        i = u // 4
                        kind, b = layout[i]
                        if kind == "p" and b < 4:
                            evac_in_window(w, b, (S["gla_qk"], 2 * w + 2) if b < 2
                                           else (S["gate_ready"], w + 1))
                        high_in_window(w, i, layout)
                        if kind == "p" and b == 5:
                            evac_in_window(w, 4, None)

            act.wait_ge(S["gla_const_in"], 64)
            nc.scalar.activation(dsumR[:], dsum[:], ACT.Copy).then_inc(S["dsum_ready"], 1)
            gla_window(0, FIRST_LAYOUT)
            with act.Fori(1, GLA) as w:
                gla_window(w, LAYOUT)

            act.wait_ge(S["dsum_done"], 12 * GLA)
            act.dma_start(bias[:], band_bias).then_inc(S["att_const_in"], 16)

            def att_window(w, last):
                v = w - GLA
                for u in range(32):
                    if u in S_AT:
                        k = S_AT[u]
                        act.wait_ge(S["neg_ready"], 8 * v + k + 1)
                        nt = (k % 4 + 1) * P
                        nc.scalar.activation(Pm[:, k % 2, 0:nt], Pm[:, k % 2, 0:nt], ACT.Exp,
                                             bias=astat[:, k % 2, 0:1], accum_out=astat[:, k % 2, 1:2])\
                            .then_inc(S["p_exp"], 1)
                    if u in T_AT:
                        k = T_AT[u]
                        act.wait_ge(S["tr_done"], 8 * v + k + 1)
                        if k >= 2:
                            act.wait_ge(S["ao_done"], 8 * v + k - 1)
                        nt = (k % 4 + 1) * P
                        nc.scalar.activation(PT[:, k % 2, 0:nt], ps[:, 6 + k % 2, 0:nt], ACT.Copy)\
                            .then_inc(S["pt_ready"], 1)
                    if u in A_AT:
                        k = A_AT[u]
                        act.wait_ge(S["ao_done"], 8 * v + k + 1)
                        if k == 0:
                            act.wait_ge(S["ol_ready"], w)
                        nc.scalar.activation(o[:, k // 4, k % 4 * P:(k % 4 + 1) * P],
                                             ps[:, 4 + k % 2, 0:P], ACT.Copy).then_inc(S["o_evac"], 1)
                    if u == PAIR_AT:
                        act.wait_ge(S["o_evac"], 16 + 8 * v + 8)
                        if last:
                            act.wait_ge(S["wout_done"], 16 * w)
                        nc.scalar.activation(oH[:], o[:], ACT.Copy).then_inc(S["oh_ready"], 1)
                    if not last:
                        load_ada(w, u)
                    if last:
                        if FILL_AT.get(u) in (7, 15):
                            d = FILL_AT[u] // 8
                            high(d, landed(FFN0 - 2 + d), S["wout_done"], 16 * (w - 1) + 8 * (d + 1))
                    elif u % 4 == 3:
                        i = u // 4
                        kind, b = LAYOUT[i]
                        if kind == "p" and b < 4:
                            evac_in_window(w, b, (S["rot_step"], 16 * v + 4 * b + 4))
                        high_in_window(w, i, LAYOUT)
                        if kind == "p" and b == 5:
                            evac_in_window(w, 4, None)

            with act.Fori(GLA, GROUPS - 1) as w:
                att_window(w, False)
            att_window(GROUPS - 1, True)
            for d in range(2):
                high(d, landed(FFN0 + d), S["wout_done"], 16 * (GROUPS - 1) + 8 * (d + 1))

            def norm_steps(j):
                nc.scalar.activation(root1[:, j:j + 1], vecs[:, V_EPS:V_EPS + 1], ACT.Sqrt)
                for k in range(KT):
                    act.wait_ge(S["cz_ready"], KT * j + k + 1)
                    if k >= 8:
                        act.wait_ge(S["var_done"], VAR_STEPS * j + k // 2 - 3)
                    nc.scalar.activation(ring_n[k % 8][:], res[:, k, :], ACT.Square)\
                        .then_inc(S["csq_ready"], 1)
                act.wait_ge(S["var_done"], VAR_STEPS * (j + 1))
                nc.scalar.activation(rstd[:], ps[:, (5, 1)[j], :], ACT.Sqrt, bias=vecs[:, V_EPS + 1:V_EPS + 2])\
                    .then_inc(S["sd_ready"], 1)

            norm_steps(0)
            for k in range(KT):
                act.wait_ge(S["n_ready"], k + 1)
                nc.scalar.activation(uH[:, k, :], ring_n[k % 8][:], ACT.Identity,
                                     bias=lnA[:, 1, k:k + 1]).then_inc(S["u2h_ready"], 1)

            def high_at(g, i):
                m = FFN0 - 2 + i
                if i < 2 or i > 5:
                    freed, count = S["up_done"], 8 * g + ((i if i < 2 else i - 4) + 1)
                else:
                    freed, count = S["down_done"], 16 * g + (4 * (i - 1) - 16)
                high(m % 2, 96 * g + 16 * (m // 2 + 1), freed, count)

            def conv_column(g, p, i, tap):
                return vecs[:, bass.ds(g * 32 + (V_CONV + 8 * p + 4 * i + tap), 1)]

            def base_steps(g, p, make_high):
                q = 4 * g + p
                for i in range(2):
                    make_high(i)
                    act.wait_ge(S["up_done"], 2 * q + (i + 1))
                    if p >= 2 or not isinstance(g, int):
                        act.wait_ge(S["pr_ready"], q - 1)
                    nc.scalar.activation((yv, yg)[i][:, p % 2, :], ps[:, 2 * (p % 2) + i, :], ACT.Identity,
                                         scale=conv_column(g, p, i, 2), bias=conv_column(g, p, i, 3))\
                        .then_inc(S["base_ready"], 1)
                act.wait_ge(S["conv_step"], 4 * q + 4)
                nc.scalar.activation(sgate[:, p % 2, :], yg[:, p % 2, :], ACT.Silu)\
                    .then_inc(S["sil_ready"], 1)

            def v_high(g, p):
                act.wait_ge(S["pr_ready"], 4 * g + (p + 1))
                nc.scalar.activation(vH[:, p, :], prod[:, p % 2, :], ACT.Copy).then_inc(S["vh_ready"], 1)

            for p in range(PAIRS):
                base_steps(0, p, lambda i: high((FFN0 + 2 * p + i) % 2, landed(FFN0 + 2 * p + i + 2),
                                                S["up_done"], 2 * p + i + 1))
                v_high(0, p)
            with act.Fori(1, FG) as g:
                base_steps(g, 0, lambda i: high_at(g, i))
                for d in range(4):
                    high_at(g, 2 + d)
                v_high(g, 0)
                for p in range(1, PAIRS):
                    base_steps(g, p, lambda i: high_at(g, 4 + 2 * p + i))
                    v_high(g, p)
            for d in range(2):
                high((NBLK - 2 + d) % 2, landed(NBLK - 2 + d), S["down_done"], 16 * (FG - 1) + 4 * (d + 1))
            norm_steps(1)
            for k in range(KT):
                if k in POOL_TILES:
                    act.wait_ge(S["pool_n_ready"], POOL_TILES.index(k) + 1)
                else:
                    act.wait_ge(S["n2_ready"], DVE_TILES.index(k) + 1)
                nc.scalar.activation(res[:, k, :], res[:, k, :], ACT.Identity,
                                     scale=vecs[:, V_LN2G + k:V_LN2G + k + 1],
                                     bias=vecs[:, V_LN2B + k:V_LN2B + k + 1]).then_inc(S["fin_ready"], 1)

        @block.vector
        def _(dve):
            V = nc.vector

            def u_low(k):
                dve.wait_ge(S["uh_ready"], k + 1)
                V.scalar_tensor_tensor(out=uL[:, k, :], in0=ring_u[k % 4][:], scalar=mod[:, k:k + 1],
                                       in1=uH[:, k, :].bitcast(F32), op0=ALU.add, op1=ALU.subtract)\
                    .then_inc(S["ul_ready"], 1)

            chain = [0]

            def pos(ins):
                chain[0] += 1
                ins.then_inc(S["pos_step"], 1)
                dve.wait_ge(S["pos_step"], chain[0])

            BIG = 1.5 * 2.0 ** 23
            TWO_PI = 2.0 * math.pi
            C1 = 6.28125
            C2 = float(np.float32(math.floor((TWO_PI - C1) * 2.0 ** 20) / 2.0 ** 20))
            C3 = float(np.float32(TWO_PI - C1 - C2))

            def angles():
                dve.wait_ge(S["pos_in"], 16)
                pos(V.tensor_copy(ang[:], posi[:]))
                pos(V.tensor_scalar(ang[:], ang[:], vecs[:, V_INVF:V_INVF + 1], None, ALU.mult))
                pos(V.tensor_scalar(turns[:], ang[:], 1.0 / TWO_PI, None, ALU.mult))
                pos(V.tensor_scalar(turns[:], turns[:], BIG, None, ALU.add))
                pos(V.tensor_scalar(turns[:], turns[:], -BIG, None, ALU.add))
                for c in (C1, C2, C3):
                    pos(V.scalar_tensor_tensor(out=ang[:], in0=turns[:], scalar=-c, in1=ang[:],
                                               op0=ALU.mult, op1=ALU.add))
                pos(V.tensor_scalar(ang[:], ang[:], math.pi, -math.pi, ALU.min, ALU.max))
                pos(V.tensor_scalar(ang[:], ang[:], 3.1415925, -3.1415925, ALU.min, ALU.max))

            def tables():
                dve.wait_ge(S["rt_ready"], 2)
                pos(V.tensor_scalar(sinT[:], sinT[:], vecs[:, V_SGN:V_SGN + 1], None, ALU.mult))
                pos(V.tensor_tensor(cosT[:], cosT[:], cosT[:], ALU.mult))
                pos(V.tensor_scalar(cosT[:], cosT[:], -2.0, 1.0, ALU.mult, ALU.add))

            V.memset(ones_row[0:1, :], 1.0).then_inc(S["ones_ready"], 1)
            dve.wait_ge(S["silu_c"], 1)
            dve.wait_ge(S["const_in"], 16)
            for k in range(KT):
                for i in range(2):
                    m = 2 * k + i
                    s = m % ADA_SLOTS
                    dve.wait_ge(ada_big_in[s], 16 * (m // ADA_SLOTS + 1))
                    V.tensor_tensor_reduce(out=ada_big[s][:], in0=ada_big[s][:], in1=csil[:], scale=1.0,
                                           scalar=0.0, op0=ALU.mult, op1=ALU.add,
                                           accum_out=mod[:, k + KT * i:k + KT * i + 1])\
                        .then_inc(S["ada_dot"], 1)
                dve.wait_ge(S["ada_dot"], 2 * k + 2)
                V.tensor_tensor(mod[:, k:k + KT + 1:KT], mod[:, k:k + KT + 1:KT], vecs[:, k:k + KT + 1:KT],
                                ALU.add).then_inc(S["mod_step"], 1)
                if k > 0:
                    u_low(k - 1)
                dve.wait_ge(S["mod_step"], k + 1)
                dve.wait_ge(x_in[k // 4], 16)
                if k >= 4:
                    dve.wait_ge(S["ul_ready"], k - 3)
                V.scalar_tensor_tensor(out=ring_u[k % 4][:], in0=res[:, k, :], scalar=mod[:, KT + k:KT + k + 1],
                                       in1=res[:, k, :], op0=ALU.mult, op1=ALU.add)\
                    .then_inc(S["uf_ready"], 1)
                if k == 2:
                    V.memset(glr[:], 1.0).then_inc(S["glr_ones"], 1)
                if k == 10:
                    angles()
                if k == 12:
                    tables()
            u_low(KT - 1)

            def ada(w, i):
                slot = i % HALF_SLOTS if isinstance(w, int) else 0
                if isinstance(w, int):
                    dve.wait_ge(ada_half_in[slot], 16 * (i // HALF_SLOTS + 1))
                else:
                    dve.wait_ge(ada_half_in[0], 256 * w + 16 * (SLOT0_LOADS - 16 + i + 1))
                V.tensor_tensor_reduce(out=ada_half[slot][:], in0=ada_half[slot][:],
                                       in1=csil[:, (i % 2) * 1024:(i % 2 + 1) * 1024], scale=1.0,
                                       scalar=0.0, op0=ALU.mult, op1=ALU.add,
                                       accum_out=acc[:, i:i + 1]).then_inc(S["ada_half_dot"], 1)

            def ada_end(w):
                n = 16 if isinstance(w, int) else 8
                dve.wait_ge(S["ada_half_dot"], 16 * w + 32)
                V.tensor_tensor(acc16[:, 0:n], acc[:, 0:2 * n:2], acc[:, 1:2 * n:2], ALU.add)\
                    .then_inc(S["mod_step"], 1)
                dve.wait_ge(S["mod_step"], 2 * w + (KT + 1))
                if isinstance(w, int):
                    V.scalar_tensor_tensor(out=mod1[:, 0, :], in0=acc16[:], scalar=1.0,
                                           in1=vecs[:, GATE1:GATE1 + KT], op0=ALU.add, op1=ALU.add)\
                        .then_inc(S["mod_step"], 1)
                else:
                    V.tensor_tensor(mod[:, bass.ds(w * 8 + (SHIFT2 - 8), 8)], acc16[:, 0:8],
                                    vecs[:, bass.ds(w * 8 + (SHIFT2 - 8), 8)], ALU.add)\
                        .then_inc(S["mod_step"], 1)
                dve.wait_ge(S["mod_step"], 2 * w + (KT + 2))

            def add_y(g, f):
                dve.wait_ge(S["wout_done"], 16 * g + f + 1)
                dve.wait_ge(S["y_added"], 16 * g)
                V.scalar_tensor_tensor(out=res[:, f, :], in0=ps[:, (f + 1) % 2, :], scalar=mod1[:, 0, f:f + 1],
                                       in1=res[:, f, :], op0=ALU.mult, op1=ALU.add)\
                    .then_inc(S["y_added"], 1)

            def in_unit(w, u, layout, ada_units):
                if layout[u // 4][0] == "o":
                    for f in (2 * (u - 4), 2 * (u - 4) + 1):
                        dve.wait_ge(S["wout_done"], 16 * w + (f - 15))
                        V.scalar_tensor_tensor(out=res[:, f, :], in0=ps[:, (f + 1) % 2, :],
                                               scalar=mod1[:, 0, f:f + 1], in1=res[:, f, :],
                                               op0=ALU.mult, op1=ALU.add).then_inc(S["y_added"], 1)
                for i, at in enumerate(ada_units):
                    if at == u:
                        ada(w, i)

            def gla_window(w, layout, ada_units):
                units = 4 * len(layout)
                for u in range(units):
                    if u == 0:
                        dve.wait_ge(S["proj_evac"], 5 * w + 2)
                        V.tensor_scalar(qw[:], stage[:, 0, :], SCALE, None, ALU.mult)\
                            .then_inc(S["gla_qk"], 1)
                        V.tensor_copy(kw[:], stage[:, 1, :]).then_inc(S["gla_qk"], 1)
                    if u == LOGITS_AT[len(layout)] + 1:
                        dve.wait_ge(S["softp_ready"], w + 1)
                        V.scalar_tensor_tensor(out=la[:].rearrange("p t f -> p (t f)"), in0=ps[:, 4, :],
                                               scalar=0.0, in1=absz[:], op0=ALU.min, op1=ALU.subtract)\
                            .then_inc(S["la_ready"], 1)
                        dve.wait_ge(S["lah_ready"], w + 1)
                        if not isinstance(w, int):
                            dve.wait_ge(S["dsum_done"], 12 * w)
                        V.tensor_tensor(laL[:], la[:], laH[:].bitcast(F32), ALU.subtract)\
                            .then_inc(S["lal_ready"], 1)
                    c, step = (u - GLA_AT) // 4, (u - GLA_AT) % 4
                    cc = 4 * w + c
                    tok = slice(c * P, (c + 1) * P)

                    def scaled(j):
                        q_c, k_c = qw[:, tok], kw[:, tok]
                        dve.wait_ge(S["exp_ready"], 3 * cc + j + 1)
                        if j < 2:
                            sets = slice(3 * j, 3 * j + 3)
                            V.tensor_tensor(Q[:, sets, :], KE[:, sets, :],
                                            q_c.unsqueeze(1).to_broadcast([P, 3, P]), ALU.mult)\
                                .then_inc(S["qk_scaled"], 1)
                            kset = KE[:, sets, :]
                            n = 3
                        else:
                            if c > 0:
                                dve.wait_ge(S["gla_o_done"], cc)
                            V.tensor_tensor(Q[:, 6:9:2, :], KE[:, 6:8, :],
                                            q_c.unsqueeze(1).to_broadcast([P, 2, P]), ALU.mult)\
                                .then_inc(S["qk_scaled"], 1)
                            kset = KE[:, 6:9:2, :]
                            n = 2
                        dve.wait_ge(S["qk_scaled"], 6 * cc + 2 * j + 1)
                        V.tensor_tensor(kset, kset, k_c.unsqueeze(1).to_broadcast([P, n, P]), ALU.mult)\
                            .then_inc(S["qk_scaled"], 1)

                    def mask(j):
                        sets = slice(3 * j, min(3 * j + 3, 8))
                        n = 3 if j < 2 else 2
                        dve.wait_ge(S["score_done"], 3 * cc + j + 1)
                        V.tensor_tensor(Q[:, sets, :],
                                        ps[:, 6 + j % 2, 0:n * P].rearrange("p (s t) -> p s t", s=n),
                                        masks[:, sets, :], ALU.mult).then_inc(S["masked"], 1)

                    def state_step(c):
                        dve.wait_ge(S["upd_done"], 3 * w + c + 1)
                        if c == 0:
                            V.tensor_copy(state[:], ps[:, 2, 0:GW]).then_inc(S["state_ready"], 1)
                        else:
                            V.scalar_tensor_tensor(out=state[:], in0=state[:], scalar=KE[:, 7, P - 1:P],
                                                   in1=ps[:, 2, 0:GW], op0=ALU.mult, op1=ALU.add)\
                                .then_inc(S["state_ready"], 1)
                        dve.wait_ge(S["state_ready"], 3 * w + c + 1)

                    if 1 <= c <= 3 and step == 0:
                        dve.wait_ge(S["ssum_ready"], cc)
                        state_step(c - 1)
                    if 0 <= c < 4:
                        if step == 0:
                            scaled(0)
                            scaled(1)
                        elif step == 1:
                            scaled(2)
                            mask(0)
                        elif step == 2:
                            mask(1)
                        else:
                            mask(2)
                            dve.wait_ge(S["masked"], 3 * cc + 3)
                            if c > 0:
                                dve.wait_ge(S["gla_o_done"], cc)
                            V.tensor_reduce(out=ssum[:], in_=Q[:, 0:8, :].rearrange("p s t -> p t s"),
                                            op=ALU.add, axis=AX_X).then_inc(S["ssum_ready"], 1)
                    if u == SQ_AT:
                        dve.wait_ge(S["sq_ready"], w + 1)
                        V.tensor_tensor(osq[:, 0, :], osq[:, 0, :], osq[:, 1, :], ALU.add)\
                            .then_inc(S["sq_added"], 1)
                    if u == MS_AT:
                        dve.wait_ge(S["rt_ready"], w + 3)
                        V.reciprocal(rms[:], rms[:]).then_inc(S["rstd_ready"], 1)
                        dve.wait_ge(S["rstd_ready"], w + 1)
                        V.tensor_tensor(o[:], o[:], rms[:].unsqueeze(1).to_broadcast([P, 2, T]), ALU.mult)\
                            .then_inc(S["o_step"], 1)
                        dve.wait_ge(S["o_step"], 3 * w + 1)
                        dve.wait_ge(S["gate_ready"], w + 1)
                        for d in range(2):
                            V.scalar_tensor_tensor(out=o[:, d, :], in0=o[:, d, :],
                                                   scalar=vecs[:, V_GNORM + d:V_GNORM + d + 1],
                                                   in1=sg[:, d, :], op0=ALU.mult, op1=ALU.mult)\
                                .then_inc(S["o_step"], 1)
                    if u == (units - 1 if layout is FIRST_LAYOUT else O_AT + 1):
                        if layout is FIRST_LAYOUT:
                            in_unit(w, u, layout, ada_units)
                            ada_end(w)
                        dve.wait_ge(S["oh_ready"], w + 1)
                        V.tensor_tensor(oL[:], o[:], oH[:].bitcast(F32), ALU.subtract)\
                            .then_inc(S["ol_ready"], 1)
                        if layout is FIRST_LAYOUT:
                            continue
                    in_unit(w, u, layout, ada_units)
                if layout is LAYOUT:
                    ada_end(w)

            gla_window(0, FIRST_LAYOUT, ADA_FIRST_AT)
            dve.wait_ge(S["ax_ready"], KT)
            with dve.Fori(1, GLA) as w:
                gla_window(w, LAYOUT, [at + 1 for at in ADA_AT])

            def rotary(v, t):
                src, dst, tmp = stage[:, t, :], rot[:, t, :], rtmp[:, t % 2, :]
                s = SCALE if t % 2 == 0 else 1.0
                if t >= 2:
                    dve.wait_ge(S["rot_step"], 16 * v + 4 * (t - 1))
                V.scalar_tensor_tensor(out=dst, in0=src, scalar=s, in1=cosT[:], op0=ALU.mult,
                                       op1=ALU.mult).then_inc(S["rot_step"], 1)
                for lo, hi in ((0, 64), (64, 0)):
                    V.scalar_tensor_tensor(out=rtmp[lo:lo + 64, t % 2, :], in0=stage[hi:hi + 64, t, :],
                                           scalar=s, in1=sinT[hi:hi + 64, :], op0=ALU.mult,
                                           op1=ALU.mult).then_inc(S["rot_step"], 1)
                dve.wait_ge(S["rot_step"], 16 * v + 4 * t + 3)
                V.tensor_tensor(dst, dst, tmp, ALU.add).then_inc(S["rot_step"], 1)

            def att_window(w, last):
                v = w - GLA
                for u in range(32):
                    if not last and u in ROT_AT:
                        t = ROT_AT[u]
                        dve.wait_ge(S["proj_evac"], 5 * w + (6 + t))
                        dve.wait_ge(S["s_done"], 8 * v + 4 * (t // 2 + 1))
                        rotary(v + 1, t)
                    if u in S_AT:
                        k = S_AT[u]
                        nt = (k % 4 + 1) * P
                        dve.wait_ge(S["s_done"], 8 * v + k + 1)
                        if k >= 2:
                            dve.wait_ge(S["tr_done"], 8 * v + k - 1)
                            dve.wait_ge(S["p_step"], 16 * v + 2 * k - 2)
                        V.tensor_tensor(Pm[:, k % 2, 0:nt], ps[:, 4 + k % 2, 0:nt], bias[:, T - nt:T], ALU.add)\
                            .then_inc(S["biased"], 1)
                        dve.wait_ge(S["biased"], 8 * v + k + 1)
                        V.tensor_reduce(out=astat[:, k % 2, 0:1], in_=Pm[:, k % 2, 0:nt], op=ALU.max,
                                        axis=AX_X, negate=True).then_inc(S["neg_ready"], 1)
                    if u + 1 in T_AT:
                        k = T_AT[u + 1]
                        nt = (k % 4 + 1) * P
                        dve.wait_ge(S["p_exp"], 8 * v + k + 1)
                        V.reciprocal(astat[:, k % 2, 2:3], astat[:, k % 2, 1:2]).then_inc(S["p_step"], 1)
                        dve.wait_ge(S["p_step"], 16 * v + 2 * k + 1)
                        V.tensor_scalar(Pm[:, k % 2, 0:nt], Pm[:, k % 2, 0:nt], astat[:, k % 2, 2:3],
                                        None, ALU.mult).then_inc(S["p_step"], 1)
                    if u == PAIR_AT:
                        dve.wait_ge(S["oh_ready"], w + 1)
                        V.tensor_tensor(oL[:], o[:], oH[:].bitcast(F32), ALU.subtract)\
                            .then_inc(S["ol_ready"], 1)
                    if last:
                        if u in FILL_AT:
                            add_y(w - 1, FILL_AT[u])
                    else:
                        in_unit(w, u, LAYOUT, [at + 1 for at in ADA_AT])
                if not last:
                    ada_end(w)

            dve.wait_ge(S["proj_evac"], 5 * GLA + 4)
            for t in range(4):
                rotary(0, t)
            dve.wait_ge(S["att_const_in"], 32)
            with dve.Fori(GLA, GROUPS - 1) as w:
                att_window(w, False)
            V.tensor_scalar(mod1[:, 1, :], mod[:, SCALE2:SCALE2 + KT], 1.0, None, ALU.add)\
                .then_inc(S["ln_vec"], 1)
            V.tensor_scalar(mod1[:, 2, :], mod[:, GATE2:GATE2 + KT], 1.0, None, ALU.add)\
                .then_inc(S["ln_vec"], 1)
            dve.wait_ge(S["ln_vec"], 2)
            V.tensor_tensor(lnA[:, 0, :], vecs[:, V_LN1G:V_LN1G + KT], mod1[:, 1, :], ALU.mult)\
                .then_inc(S["ln_vec"], 1)
            V.tensor_tensor(lnA[:, 1, :], vecs[:, V_LN1B:V_LN1B + KT], mod1[:, 1, :], ALU.mult)\
                .then_inc(S["ln_vec"], 1)
            dve.wait_ge(S["ln_vec"], 4)
            V.tensor_tensor(lnA[:, 1, :], lnA[:, 1, :], mod[:, SHIFT2:SHIFT2 + KT], ALU.add)\
                .then_inc(S["ln_vec"], 1)
            V.tensor_scalar(lnA[:, 2, :], vecs[:, V_LN1G:V_LN1G + KT], ALPHA, None, ALU.mult)\
                .then_inc(S["ln_vec"], 1)
            V.tensor_scalar(lnA[:, 3, :], vecs[:, V_LN1B:V_LN1B + KT], ALPHA, None, ALU.mult)\
                .then_inc(S["ln_vec"], 1)
            dve.wait_ge(S["ln_vec"], 7)
            att_window(GROUPS - 1, True)

            def add_tile(j, f, source, count):
                dve.wait_ge(source, count + f + 1)
                if f == 9:
                    first = res[:, 8, :]
                else:
                    dve.wait_ge(S["zsum2_step"], 7 * j + f - 9)
                    first = zsum[:, 1, :]
                V.tensor_tensor(zsum[:, 1, :], first, res[:, f, :], ALU.add).then_inc(S["zsum2_step"], 1)

            for f in range(KT):
                add_y(GROUPS - 1, f)
                if f > 8:
                    add_tile(0, f, S["y_added"], 16 * (GROUPS - 1))

            def norm_steps(j):
                dve.wait_ge(S["sum_done"], j + 1)
                for k in range(KT):
                    V.tensor_tensor(res[:, k, :], res[:, k, :], ps[:, (4, 0)[j], :], ALU.subtract)\
                        .then_inc(S["cz_ready"], 1)
                dve.wait_ge(S["sd_ready"], j + 1)
                V.reciprocal(rstd[:], rstd[:]).then_inc(S["lnr_ready"], 1)
                dve.wait_ge(S["lnr_ready"], j + 1)

            dve.wait_ge(S["y_added"], 16 * GROUPS)
            norm_steps(0)

            def u2_low(k):
                dve.wait_ge(S["u2h_ready"], k + 1)
                V.scalar_tensor_tensor(out=uL[:, k, :], in0=ring_n[k % 8][:], scalar=lnA[:, 1, k:k + 1],
                                       in1=uH[:, k, :].bitcast(F32), op0=ALU.add, op1=ALU.subtract)\
                    .then_inc(S["u2l_ready"], 1)

            for k in range(KT):
                if k >= 8:
                    dve.wait_ge(S["u2l_ready"], k - 7)
                V.scalar_tensor_tensor(out=ring_n[k % 8][:], in0=res[:, k, :], scalar=lnA[:, 0, k:k + 1],
                                       in1=rstd[:], op0=ALU.mult, op1=ALU.mult).then_inc(S["n_ready"], 1)
                if k >= 1:
                    u2_low(k - 1)
            u2_low(KT - 1)
            for k in range(KT):
                V.scalar_tensor_tensor(out=res[:, k, :], in0=res[:, k, :], scalar=lnA[:, 2, k:k + 1],
                                       in1=rstd[:], op0=ALU.mult, op1=ALU.mult).then_inc(S["z2_step"], 1)
                if k >= 1:
                    dve.wait_ge(S["z2_step"], k)
                    V.tensor_scalar(res[:, k - 1, :], res[:, k - 1, :], lnA[:, 3, k - 1:k], None, ALU.add)\
                        .then_inc(S["z2_added"], 1)
            dve.wait_ge(S["z2_step"], KT)
            V.tensor_scalar(res[:, KT - 1, :], res[:, KT - 1, :], lnA[:, 3, KT - 1:KT], None, ALU.add)\
                .then_inc(S["z2_added"], 1)

            def pair_steps(g, p):
                q = 4 * g + p
                for i in range(2):
                    dve.wait_ge(S["base_ready"], 2 * q + i + 1)
                    dst = yv if i == 0 else yg
                    for tap, lag in ((1, 1), (0, 2)):
                        col = V_CONV + 4 * i + 8 * p + tap
                        w = vecs[:, bass.ds(g * 32 + col, 1)]
                        if lag == 2:
                            dve.wait_ge(S["conv_step"], 4 * q + 2 * i + 1)
                        V.scalar_tensor_tensor(out=dst[:, p % 2, lag:T], in0=ps[:, 2 * (p % 2) + i, 0:T - lag],
                                               scalar=w, in1=dst[:, p % 2, lag:T], op0=ALU.mult,
                                               op1=ALU.add).then_inc(S["conv_step"], 1)
                dve.wait_ge(S["sil_ready"], q + 1)
                if p >= 2 or not isinstance(g, int):
                    dve.wait_ge(S["vl_ready"], q - 1)
                V.tensor_tensor(prod[:, p % 2, :], yv[:, p % 2, :], sgate[:, p % 2, :], ALU.mult)\
                    .then_inc(S["pr_ready"], 1)

            def pair_low(g, p):
                q = 4 * g + p
                dve.wait_ge(S["vh_ready"], q + 1)
                V.tensor_tensor(vL[:, p, :], prod[:, p % 2, :], vH[:, p, :].bitcast(F32), ALU.subtract)\
                    .then_inc(S["vl_ready"], 1)

            def down_steps(g, last=False):
                for f in range(KT):
                    dve.wait_ge(S["down_done"], 16 * g + f + 1)
                    dve.wait_ge(S["z2_added"], 16 * g + KT)
                    V.scalar_tensor_tensor(out=res[:, f, :], in0=ps[:, 4 + f % 4, :],
                                           scalar=mod1[:, 2, f:f + 1], in1=res[:, f, :], op0=ALU.mult,
                                           op1=ALU.add).then_inc(S["z2_added"], 1)
                    if last and f > 8:
                        add_tile(1, f, S["z2_added"], 16 * FG)

            for p in range(PAIRS):
                pair_steps(0, p)
                pair_low(0, p)
            with dve.Fori(1, FG) as g:
                pair_steps(g, 0)
                down_steps(g - 1)
                pair_low(g, 0)
                for p in range(1, PAIRS):
                    pair_steps(g, p)
                    pair_low(g, p)
            down_steps(FG - 1, True)
            dve.wait_ge(S["z2_added"], 16 * FG + KT)
            norm_steps(1)
            for k in DVE_TILES:
                V.tensor_tensor(res[:, k, :], res[:, k, :], rstd[:], ALU.mult).then_inc(S["n2_ready"], 1)

        @block.tensor
        def _(pe):
            def w3(s, n, cols):
                return (wH[s][:].rearrange("p (k n) -> p k n", n=cols),
                        wL[s][:].rearrange("p (k n) -> p k n", n=cols))

            def quarter(bank, s, kq):
                h, l = w3(s, KT, P)
                for k in range(4 * kq, 4 * kq + 4):
                    last = three(bank, h[:, k, :], l[:, k, :], uH[:, k, :], uL[:, k, :],
                                 k == 0, k == KT - 1)
                return last

            def values(k, h, l):
                for t in range(TT):
                    tok = slice(t * P, (t + 1) * P)
                    bank = ps[:, 2 + t // 2, (t % 2) * GW:(t % 2 + 1) * GW]
                    nc.tensor.matmul(bank, uH[:, k, tok], h, start=(k == 0 and t % 2 == 0),
                                     stop=False, skip_group_check=True)
                    nc.tensor.matmul(bank, uL[:, k, tok], h, start=False, stop=False,
                                     skip_group_check=True)
                    last = nc.tensor.matmul(bank, uH[:, k, tok], l, start=False,
                                            stop=(k == KT - 1), skip_group_check=True)
                return last

            def keep_warm(n):
                for _ in range(n):
                    nc.tensor.matmul(ps[:, 7, :], ones_ln[:], csil[:, 0:T], start=True, stop=True)

            pe.wait_ge(S["c_in"], 16)
            pe.wait_ge(S["ones_ready"], 1)
            for b in range(4):
                last = nc.tensor.matmul(ps[:, b, :], ones_row[0:1, :], c_row[0:1, b * T:(b + 1) * T],
                                        start=True, stop=True)
            last.then_inc(S["c_spread"], 1)

            for k in range(KT):
                n = k // 2
                if k % 2 == 0:
                    pe.wait_ge(S["w_lo"], n + 1)
                pe.wait_ge(S["ul_ready"], k + 1)
                h, l = (x[n % 2][:, 0:2 * FIRST_W].rearrange("p (k n) -> p k n", k=2)[:, k % 2, :]
                        for x in (wH, wL))
                for bank, at, m in ((0, 0, P), (1, P, P), (7, 6 * P, RANK), (2, 4 * P, GW),
                                    (4, 2 * P, P), (5, 3 * P, P)):
                    if bank == 2:
                        last = values(k, h[:, at:at + GW], l[:, at:at + GW])
                    else:
                        last = three(ps[0:m, bank, :], h[:, at:at + m], l[:, at:at + m], uH[:, k, :],
                                     uL[:, k, :], k == 0, k == KT - 1)
                    if k == KT - 1:
                        last.then_inc(S["first_done"], 1)
                if k % 2 == 1 and k < KT - 1:
                    last.then_inc(S["first_used"], 1)

            def projection_unit(w, u, i, b):
                kq = u % 4
                s = i % 2
                if kq == 0:
                    first = isinstance(w, int)
                    pe.wait_ge(S["w_lo"], PRO + i + 1 if first else 8 * w + (7 + i))
                    if b == 0:
                        pe.wait_ge(S["proj_evac"], 1 if first else 5 * w + 3)
                    elif b == 1 and first:
                        pe.wait_ge(S["proj_evac"], 2)
                    elif b == 2 and first:
                        pe.wait_ge(S["proj_evac"], 6)
                    elif b < 3:
                        pe.wait_ge(S["y_added"], 16 * w + (b - 2))
                    elif b == 3:
                        pe.wait_ge(S["proj_evac"], 5 * w + 7)
                    elif b == 4:
                        pe.wait_ge(S["proj_evac"], 5 * w + 5)
                if b < 4:
                    last = quarter(ps[:, b % 2, :], s, kq)
                else:
                    h, l = w3(s, 8, GW)
                    for kk in range(2 * kq, 2 * kq + 2):
                        last = values(8 * (b - 4) + kk, h[:, kk, :], l[:, kk, :])
                if kq == 3:
                    last.then_inc(S["proj_done"], 1)

            def wout(f, s, block, free, count):
                if f % 8 == 0:
                    pe.wait_ge(S["w_lo"], block)
                pe.wait_ge(free, count)
                h, l = (x[s][:].rearrange("p (k f n) -> p k f n", k=2, f=8) for x in (wH, wL))
                for k in range(2):
                    last = three(ps[:, (f + 1) % 2, :], h[:, k, f % 8, :], l[:, k, f % 8, :], oH[:, k, :],
                                 oL[:, k, :], k == 0, k == 1)
                last.then_inc(S["wout_done"], 1)

            def unit(w, u, layout):
                i = u // 4
                kind, b = layout[i]
                if kind == "p":
                    projection_unit(w, u, i, b)
                else:
                    if u == 4:
                        pe.wait_ge(S["ol_ready"], w)
                    for f in (2 * (u - 4), 2 * (u - 4) + 1):
                        if f < 2:
                            free, count = S["proj_evac"], 5 * w + (4 + 2 * f)
                        else:
                            free, count = S["y_added"], 16 * w + (f - 17)
                        wout(f, i % 2, 8 * w + (7 + i), free, count)

            def decays(w, c, j):
                cc = 4 * w + c
                if c == 0 and j < 2:
                    pe.wait_ge(S["lal_ready"], w + 1)
                    if isinstance(w, int):
                        pe.wait_ge(S["gla_const_in"], 64)
                        pe.wait_ge(S["dsum_ready"], 1)
                elif j < 2:
                    pe.wait_ge(S["exp_ready"], 3 * cc)
                else:
                    pe.wait_ge(S["exp_ready"], 3 * cc + 1)
                spans = dsumR[:, 3 * j:3 * j + 3, :].rearrange("p s t -> p (s t)")
                nc.tensor.matmul(ps[:, 4 + j % 2, 0:3 * P], laH[:, c, :], spans, start=True, stop=False)
                nc.tensor.matmul(ps[:, 4 + j % 2, 0:3 * P], laL[:, c, :], spans, start=False, stop=True)\
                    .then_inc(S["dsum_done"], 1)

            def scores(w, c, j):
                cc = 4 * w + c
                pe.wait_ge(S["qk_scaled"], 6 * cc + 2 * j + 2)
                if j == 0 and c > 0:
                    pe.wait_ge(S["masked"], 3 * cc)
                if j == 1 and c > 0:
                    pe.wait_ge(S["o_evac"], cc)
                if j == 2:
                    pe.wait_ge(S["masked"], 3 * cc + 1)
                tok = slice(c * P, (c + 1) * P)
                pairs = [(KE[:, 3 * j + i, :], Q[:, 3 * j + i, :]) for i in range(3 if j < 2 else 1)]
                if j == 2:
                    pairs.append((kw[:, tok], qw[:, tok]))
                for i, (k, q) in enumerate(pairs):
                    last = nc.tensor.matmul(ps[:, 6 + j % 2, i * P:(i + 1) * P], k, q, start=True, stop=True,
                                            skip_group_check=True)
                last.then_inc(S["score_done"], 1)

            def gla_output(w, c):
                cc = 4 * w + c
                pe.wait_ge(S["ssum_ready"], cc + 1)
                if c > 0:
                    pe.wait_ge(S["state_ready"], 3 * w + c)
                else:
                    pe.wait_ge(S["proj_evac"], 5 * w + 5)
                for d in range(2):
                    dv = slice(d * P, (d + 1) * P)
                    last = nc.tensor.matmul(ps[:, 7, dv], Vw[:, c, dv], ssum[:], start=True,
                                            stop=(c == 0), skip_group_check=True)
                    if c > 0:
                        last = nc.tensor.matmul(ps[:, 7, dv], state[:, dv], Q[:, 8, :], start=False,
                                                stop=True, skip_group_check=True)
                last.then_inc(S["gla_o_done"], 1)
                if c < 3:
                    pe.wait_ge(S["kht_ready"], 3 * w + c + 1)
                    nc.tensor.matmul(ps[:, 2, 0:GW], khT[:], Vw[:, c, :], start=True, stop=True)\
                        .then_inc(S["upd_done"], 1)

            def gla_window(w, layout):
                for u in range(4 * len(layout)):
                    if u == LOGITS_AT[len(layout)]:
                        pe.wait_ge(S["wgate_in"], 16 * w + 16)
                        pe.wait_ge(S["glr_ready"], 1)
                        if isinstance(w, int):
                            pe.wait_ge(S["proj_evac"], 5)
                        for t in range(TT):
                            last = nc.tensor.matmul(ps[:, 4, t * P:(t + 1) * P], glr[:, t * P:(t + 1) * P],
                                                    wgate[:], start=True, stop=True, skip_group_check=True)
                        last.then_inc(S["logit_done"], 1)
                    c, step = (u - GLA_AT) // 4, (u - GLA_AT) % 4
                    if step == 0 and 1 <= c <= 4:
                        gla_output(w, c - 1)
                    if 0 <= c < 4:
                        if step == 0:
                            decays(w, c, 0)
                            decays(w, c, 1)
                        elif step == 1:
                            decays(w, c, 2)
                            scores(w, c, 0)
                        elif step == 2:
                            scores(w, c, 1)
                        else:
                            scores(w, c, 2)
                            if c < 3:
                                if c == 0:
                                    pe.wait_ge(S["proj_evac"], 5 * w + 5)
                                else:
                                    pe.wait_ge(S["kht_ready"], 3 * w + c)
                                nc.tensor.transpose(ps[:, 3, 0:P], KE[:, 8, :], ident[:])\
                                    .then_inc(S["kt_done"], 1)
                    if layout[u // 4] == ("p", 4) and u % 4 == 0:
                        pe.wait_ge(S["state_ready"], 3 * w + 3)
                        pe.wait_ge(S["kht_ready"], 3 * w + 3)
                    if u == MS_AT - 1:
                        pe.wait_ge(S["sq_added"], w + 1)
                        nc.tensor.matmul(ps[:, 6, :], ones_rms[:], osq[:, 0, :], start=True, stop=True)\
                            .then_inc(S["ms_done"], 1)
                    unit(w, u, layout)

            gla_window(0, FIRST_LAYOUT)
            with pe.Fori(1, GLA) as w:
                gla_window(w, LAYOUT)

            def att_window(w, is_last):
                v = w - GLA
                for u in range(32):
                    if u in S_AT:
                        k = S_AT[u]
                        h, i = k // 4, k % 4
                        pe.wait_ge(S["rot_step"], 16 * v + 8 * h + 8)
                        if k >= 2:
                            pe.wait_ge(S["o_evac"], 16 + 8 * v + k - 1)
                        nt = (i + 1) * P
                        nc.tensor.matmul(ps[:, 4 + k % 2, 0:nt], rot[:, 2 * h, i * P:nt],
                                         rot[:, 2 * h + 1, 0:nt], start=True, stop=True)\
                            .then_inc(S["s_done"], 1)
                    if u in T_AT:
                        k = T_AT[u]
                        pe.wait_ge(S["p_step"], 16 * v + 2 * k + 2)
                        if k >= 2:
                            pe.wait_ge(S["pt_ready"], 8 * v + k - 1)
                        for j in range(k % 4 + 1):
                            last = nc.tensor.transpose(ps[:, 6 + k % 2, j * P:(j + 1) * P],
                                                       Pm[:, k % 2, j * P:(j + 1) * P], ident[:])
                        last.then_inc(S["tr_done"], 1)
                    if u in A_AT:
                        k = A_AT[u]
                        h, i = k // 4, k % 4
                        pe.wait_ge(S["pt_ready"], 8 * v + k + 1)
                        if k == 0:
                            pe.wait_ge(S["proj_evac"], 5 * w + 5)
                        for j in range(i + 1):
                            last = nc.tensor.matmul(ps[:, 4 + k % 2, 0:P], Vw[:, j, h * P:(h + 1) * P],
                                                    PT[:, k % 2, j * P:(j + 1) * P], start=(j == 0),
                                                    stop=(j == i), skip_group_check=True)
                        last.then_inc(S["ao_done"], 1)
                    if not is_last:
                        unit(w, u, LAYOUT)
                    elif u in FILL_AT:
                        f = FILL_AT[u]
                        if f == 0:
                            pe.wait_ge(S["ol_ready"], w)
                        wout(f, f // 8, FFN0 - 4 + f // 8 + 1,
                             *((S["proj_evac"], 5 * w + (4 - f)) if f < 2
                               else (S["y_added"], 16 * w + (f - 17))))

            with pe.Fori(GLA, GROUPS - 1) as w:
                att_window(w, False)
            last_w = GROUPS - 1
            att_window(last_w, True)
            keep_warm(5)
            pe.wait_ge(S["ol_ready"], GROUPS)
            for f in range(KT):
                wout(f, f // 8, FFN0 - 2 + f // 8 + 1, S["y_added"], 16 * last_w + (f - 1))

            def norm_steps(j):
                pe.wait_ge(S["zsum_step"], 7 * (j + 1))
                nc.tensor.matmul(ps[:, (4, 0)[j], :], ones_ln[:], zsum[:, 0, :], start=True, stop=False)
                pe.wait_ge(S["zsum2_step"], 7 * (j + 1))
                nc.tensor.matmul(ps[:, (4, 0)[j], :], ones_ln[:], zsum[:, 1, :], start=False, stop=True)\
                    .then_inc(S["sum_done"], 1)
                for i in range(VAR_STEPS):
                    if i < SQ_PAIRS:
                        k = 2 * i
                        pe.wait_ge(S["pair_ready"], SQ_PAIRS * j + i + 1)
                    else:
                        k = SQ_PAIRS + i
                        pe.wait_ge(S["csq_ready"], KT * j + k + 1)
                    nc.tensor.matmul(ps[:, (5, 1)[j], :], ones_ln[:], ring_n[k % 8][:], start=(i == 0),
                                     stop=(i == VAR_STEPS - 1)).then_inc(S["var_done"], 1)

            norm_steps(0)
            keep_warm(7)

            def up(g, p, i, n_wait, s):
                q = 4 * g + p
                pe.wait_ge(S["w_lo"], n_wait)
                if p >= 2 or not isinstance(g, int):
                    pe.wait_ge(S["conv_step"], 4 * q + (2 * i - 6))
                h, l = w3(s, KT, P)
                bank = ps[:, 2 * (p % 2) + i, :]
                for k in range(KT):
                    last = three(bank, h[:, k, :], l[:, k, :], uH[:, k, :], uL[:, k, :], k == 0, k == KT - 1)
                last.then_inc(S["up_done"], 1)

            def down(g, n_off, last_late=False):
                def product(f, k, h, l):
                    return three(ps[:, 4 + f % 4, :], h[:, k, f % 4, :], l[:, k, f % 4, :], vH[:, k, :],
                                 vL[:, k, :], k == 0, k == PAIRS - 1)

                if last_late:
                    pe.wait_ge(S["vl_ready"], 4 * g + PAIRS - 1)
                    pe.wait_ge(S["w_lo"], 12 * g + (n_off + 1))
                    h, l = (x[n_off % 2][:].rearrange("p (k f n) -> p k f n", k=4, f=4) for x in (wH, wL))
                    for f in range(4):
                        pe.wait_ge(S["z2_added"], 16 * g + KT)
                        for k in range(PAIRS - 1):
                            product(f, k, h, l)
                pe.wait_ge(S["vl_ready"], 4 * g + PAIRS)
                for f in range(KT):
                    d = f // 4
                    s = (n_off + d) % 2
                    if f % 4 == 0:
                        pe.wait_ge(S["w_lo"], 12 * g + (n_off + d + 1))
                        h, l = (x[s][:].rearrange("p (k f n) -> p k f n", k=4, f=4) for x in (wH, wL))
                    pe.wait_ge(S["z2_added"], 16 * g + (KT if f < 4 else KT + f - 3))
                    for k in range(PAIRS - 1 if last_late and f < 4 else 0, PAIRS):
                        last = product(f, k, h, l)
                    last.then_inc(S["down_done"], 1)

            pe.wait_ge(S["w_lo"], FFN0 + 2)
            for k in range(KT):
                pe.wait_ge(S["u2l_ready"], k + 1)
                for i in range(2):
                    h, l = w3(i, KT, P)
                    last = three(ps[:, i, :], h[:, k, :], l[:, k, :], uH[:, k, :], uL[:, k, :],
                                 k == 0, k == KT - 1)
                    if k == KT - 1:
                        last.then_inc(S["up_done"], 1)
            keep_warm(6)
            for p in range(1, PAIRS):
                for i in range(2):
                    n = FFN0 + 2 * p + i
                    up(0, p, i, n + 1, n % 2)
            with pe.Fori(1, FG) as g:
                for i in range(12):
                    m = FFN0 - 4 + i
                    if 2 <= i < 6:
                        if i == 2:
                            down(g - 1, FFN0 - 4 + 2 + 12)
                        continue
                    p = 0 if i < 2 else (i - 4) // 2
                    up(g, p, i % 2, 12 * g + (m + 1), m % 2)
            down(FG - 1, FFN0 - 4 + 12, True)
            norm_steps(1)


def level_constants():
    t = np.arange(P)
    sums = np.zeros((P, SETS, P), np.float32)
    masks = np.zeros((P, LEVELS + 1, P), np.float32)
    tp = t[:, None]
    tq = t[None, :]
    for level in range(LEVELS):
        half = P >> (level + 1)
        mid = tq // (2 * half) * (2 * half) + half - 1
        late = tq % (2 * half) >= half
        span = np.where(late, (tp > mid) & (tp <= tq), (tp > tq) & (tp <= mid))
        sums[:, level, :] = span / TAU
        same = tp // (2 * half) == tq // (2 * half)
        masks[:, level, :] = same & late & (tp % (2 * half) < half)
    sums[:, LEVELS, :] = (tp <= tq) / TAU
    sums[:, LEVELS + 1, :] = (tp > tq) / TAU
    masks[:, LEVELS, :] = tp == tq
    return sums, masks


def band_constants():
    dist = (3 * P + np.arange(P))[:, None] - np.arange(T)[None, :]
    count = ((dist >= 0) & (dist <= 128)).astype(int)
    count += (dist >= 0) & (dist <= 512) & (dist % 4 == 0)
    count += (dist >= 0) & (dist <= 2048) & (dist % 16 == 0)
    return np.where(count > 0, np.log(np.maximum(count, 1)), -1e30).astype(np.float32)


def kernel(x, c, positions, w_ada, b_ada, w_in, w_gla_gate, b_gla_gate, gla_norm_g, w_out, ln1_g, ln1_b,
           w_up, conv_w, conv_b, w_down, ln2_g, ln2_b):
    import concourse.bacc as bacc
    from concourse.bass_utils import run_bass_kernel_spmd

    f32 = np.float32
    x, w_ada, w_in, w_out, w_up, w_down = (np.asarray(a) for a in (x, w_ada, w_in, w_out, w_up, w_down))
    x_t = np.ascontiguousarray(x[0].T.reshape(KT, P, T).transpose(1, 0, 2))

    def tiles(w):
        return w.reshape(-1, P, w.shape[1]).transpose(1, 0, 2)

    wi, wo, wu, wd = w_in[0], w_out[0], w_up[0], w_down[0]
    gk, ga = 4 * P, 8 * P
    off_k, off_v, off_g, off_lr = gk, 2 * gk, 2 * gk + ga, 2 * gk + 2 * ga
    off_aq = off_lr + RANK
    off_ak, off_av = off_aq + ga, off_aq + 2 * ga

    def projection(group):
        if group < GLA:
            at = [group * P, off_k + group * P, off_g + group * GW, off_g + group * GW + P]
            v = off_v + group * GW
        else:
            h = 2 * (group - GLA)
            at = [off_aq + h * P, off_ak + h * P, off_aq + (h + 1) * P, off_ak + (h + 1) * P]
            v = off_av + h * P
        blocks = [tiles(wi[:, a:a + P]) for a in at]
        values = tiles(wi[:, v:v + GW])
        return blocks + [values[:, 0:8], values[:, 8:16]]

    def output(group):
        rows = tiles(wo[group * GW:(group + 1) * GW])
        return [rows[:, :, d * 1024:(d + 1) * 1024] for d in range(2)]

    def up(f):
        return [tiles(wu[:, f * P:(f + 1) * P]), tiles(wu[:, DFF + f * P:DFF + (f + 1) * P])]

    def down(g):
        rows = tiles(wd[g * PAIRS * P:(g + 1) * PAIRS * P])
        return [rows[:, :, d * 512:(d + 1) * 512] for d in range(4)]

    columns_0 = [slice(a, a + n) for a, n in ((0, P), (off_k, P), (off_g, GW), (off_v, GW), (off_lr, RANK))]
    first = tiles(np.concatenate([wi[:, c] for c in columns_0], axis=1))
    w_first = np.ascontiguousarray(first.reshape(P, PRO, 2 * FIRST_W).transpose(1, 0, 2))
    blocks = projection(1)
    for w in range(1, GROUPS):
        if w + 1 < GROUPS:
            proj = projection(w + 1)
            blocks += proj[:1] + output(w - 1) + proj[1:]
        else:
            blocks += output(w - 1) + output(w)
    for p in range(PAIRS):
        blocks += up(p)
    for g in range(1, FG):
        blocks += up(PAIRS * g) + down(g - 1)
        for p in range(1, PAIRS):
            blocks += up(PAIRS * g + p)
    blocks += down(FG - 1)
    assert len(blocks) == NBLK - PRO
    w_stream = np.empty((NBLK - PRO, P, WBLK), f32)
    for n, b in enumerate(blocks):
        w_stream[n] = b.reshape(P, WBLK)

    w_ada_t = np.ascontiguousarray(w_ada[0].T).reshape(6 * D // P, P, D)
    w_gate = np.concatenate([np.asarray(w_gla_gate)[0], np.asarray(b_gla_gate)[0][None]])
    w_gate = np.ascontiguousarray(w_gate.reshape(RANK + 1, GLA, P).transpose(1, 0, 2))

    def columns(v):
        return np.asarray(v).reshape(-1, P).T

    vec = np.zeros((P, NVEC), f32)
    vec[:, V_BADA:V_BADA + 96] = columns(b_ada[0])
    for at, v in ((V_LN1G, ln1_g), (V_LN1B, ln1_b), (V_LN2G, ln2_g), (V_LN2B, ln2_b)):
        vec[:, at:at + KT] = columns(v[0])
    vec[:, V_GNORM:V_GNORM + 2] = columns(gla_norm_g[0])
    half = np.arange(64, dtype=f32)
    inv_freq = (f32(10000.0) ** (-half / f32(64))).astype(f32)
    vec[:, V_INVF] = np.concatenate([inv_freq, inv_freq])
    vec[:, V_SGN] = np.repeat([1.0, -1.0], 64)
    vec[:, V_EPS] = RMS_EPS
    vec[:, V_EPS + 1] = LN_EPS
    vec[:, V_EPS + 2] = 1.0
    conv = np.concatenate([np.asarray(conv_w)[0], np.asarray(conv_b)[0][None]])
    conv = conv.reshape(4, 2, FT, P).transpose(3, 2, 1, 0)
    vec[:, V_CONV:V_CONV + FT * 8] = conv.reshape(P, FT * 8)

    sums, masks = level_constants()
    eye = np.zeros((P, 3, P), f32)
    eye[:, 0, :] = np.eye(P)
    eye[:, 1, :] = 1.0 / GW
    eye[:, 2, :] = 1.0 / D
    arrays = {
        "x": x_t,
        "c_in": np.ascontiguousarray(np.asarray(c).reshape(1, D)),
        "pos_rows": np.ascontiguousarray(np.broadcast_to(np.asarray(positions)[0], (P, T))),
        "w_first": w_first, "w_stream": w_stream, "w_ada_t": w_ada_t, "w_gate": w_gate, "vec": vec,
        "decay_sums": sums, "level_masks": masks, "band_bias": band_constants(), "eye": eye,
    }
    nc = bacc.Bacc("TRN2", target_bir_lowering=False, num_devices=1, dynamic_dma_scratch_size=1024)
    args = [nc.dram_tensor(n, a.shape, mybir.dt.from_np(a.dtype), kind="ExternalInput").ap()
            for n, a in arrays.items()]
    out = nc.dram_tensor("out", (P, KT, T), F32, kind="ExternalOutput").ap()
    build(nc, *args, out)
    got = run_bass_kernel_spmd(nc, [arrays], core_ids=[0]).results[0]["out"]
    return np.ascontiguousarray(got.transpose(1, 0, 2).reshape(D, T).T)[None]
```
